# Optimizing a Trainium2 kernel written in Bass

```python
import jax, jax.numpy as jnp
from jax import lax
import numpy as np

D_MODEL = 1024
BATCH = 1
SEQ = 256
DEPTH = 1

D_MIX = D_MODEL
GLA_HEADS = 4
GLA_HEAD_V = (D_MIX // 2) // GLA_HEADS
GLA_HEAD_K = GLA_HEAD_V // 2
GLA_GATE_RANK = 16
GLA_GATE_TAU = 16.0
GLA_CHUNK = 64
MOBA_HEADS = 4
MOBA_HEAD_DIM = (D_MIX - GLA_HEADS * GLA_HEAD_V) // MOBA_HEADS
MOBA_BLOCK = 256
MOBA_TOPK = 3
MOBA_QUERY_GROUP = 8
ROPE_THETA = 10000.0
D_FF = -(-8 * D_MODEL // (3 * 256)) * 256
EPS = 1e-6

GLA_QK = GLA_HEADS * GLA_HEAD_K
GLA_V = GLA_HEADS * GLA_HEAD_V
MOBA_W = MOBA_HEADS * MOBA_HEAD_DIM
IN_SIZES = (GLA_QK, GLA_QK, GLA_V, GLA_V, GLA_GATE_RANK, MOBA_W, MOBA_W, MOBA_W)
IN_OFFSETS = tuple(int(o) for o in np.cumsum((0,) + IN_SIZES))
D_IN_PROJ = IN_OFFSETS[-1]

kernel_name = "hymba_gla_moba_hybrid_block"

def rms_norm(x, gain):
    xf = x.astype(jnp.float32)
    y = xf * lax.rsqrt(jnp.mean(xf * xf, axis=-1, keepdims=True) + EPS)
    return (y * gain.astype(jnp.float32)).astype(x.dtype)

def rotary(x, positions):
    half = x.shape[-1] // 2
    inv_freq = jnp.power(ROPE_THETA, -jnp.arange(half, dtype=jnp.float32) / half)
    ang = positions.astype(jnp.float32)[:, :, None] * inv_freq
    cos = jnp.cos(ang)[:, None]
    sin = jnp.sin(ang)[:, None]
    xf = x.astype(jnp.float32)
    x1, x2 = xf[..., :half], xf[..., half:]
    return jnp.concatenate([x1 * cos - x2 * sin, x2 * cos + x1 * sin], axis=-1).astype(x.dtype)

def gla_chunked(q, k, v, log_a):
    B, H, S, dk = q.shape
    dv = v.shape[-1]
    nc = S // GLA_CHUNK
    rs = lambda t: t.reshape(B, H, nc, GLA_CHUNK, t.shape[-1])
    q = rs(q) * (dk ** -0.5)
    k = rs(k)
    v = rs(v)
    b = jnp.cumsum(rs(log_a), axis=3)
    b_last = b[:, :, :, -1:, :]
    q_dec = q * jnp.exp(b)
    k_inv = k * jnp.exp(-b)
    causal = jnp.tril(jnp.ones((GLA_CHUNK, GLA_CHUNK), dtype=bool))
    a = jnp.where(causal, jnp.einsum('bhncd,bhnsd->bhncs', q_dec, k_inv), 0.0)
    o_intra = jnp.einsum('bhncs,bhnsv->bhncv', a, v)
    k_to_end = k * jnp.exp(b_last - b)
    u = jnp.einsum('bhncd,bhncv->bhndv', k_to_end, v)
    chunk_decay = jnp.exp(b_last[:, :, :, 0, :])

    def step(state, inp):
        d, u_c = inp
        return d[..., None] * state + u_c, state

    _, s_prev = lax.scan(step, jnp.zeros((B, H, dk, dv), jnp.float32),
                         (jnp.moveaxis(chunk_decay, 2, 0), jnp.moveaxis(u, 2, 0)))
    s_prev = jnp.moveaxis(s_prev, 0, 2)
    o_inter = jnp.einsum('bhncd,bhndv->bhncv', q_dec, s_prev)
    return (o_intra + o_inter).reshape(B, H, S, dv)

def moba_attention(q, k, v):
    B, H, S, dh = q.shape
    nb = -(-S // MOBA_BLOCK)
    s_pad = nb * MOBA_BLOCK
    pad = ((0, 0), (0, 0), (0, s_pad - S), (0, 0))
    q_p, k_p, v_p = jnp.pad(q, pad), jnp.pad(k, pad), jnp.pad(v, pad)
    kb = k_p.reshape(B, H, nb, MOBA_BLOCK, dh)
    vb = v_p.reshape(B, H, nb, MOBA_BLOCK, dh)
    k_mean = jnp.mean(kb.astype(jnp.float32), axis=3)
    gate = jnp.einsum('bhsd,bhnd->bhsn', q_p.astype(jnp.float32), k_mean)
    q_blk = jnp.arange(s_pad) // MOBA_BLOCK
    past = jnp.arange(nb)[None, :] < q_blk[:, None]
    gate = jnp.where(past, gate, -jnp.inf)
    top = min(MOBA_TOPK, nb)
    _, sel = lax.top_k(gate, top)
    sel_valid = sel < q_blk[None, None, :, None]
    scale = dh ** -0.5
    bi = jnp.arange(B)[:, None, None, None]
    hi = jnp.arange(H)[None, :, None, None]
    G = MOBA_QUERY_GROUP

    def group(gi):
        start = gi * G
        qg = lax.dynamic_slice_in_dim(q_p, start, G, axis=2)
        selg = lax.dynamic_slice_in_dim(sel, start, G, axis=2)
        validg = lax.dynamic_slice_in_dim(sel_valid, start, G, axis=2)
        k_sel = kb[bi, hi, selg]
        v_sel = vb[bi, hi, selg]
        s_sel = jnp.einsum('bhgd,bhgnkd->bhgnk', qg, k_sel).astype(jnp.float32) * scale
        s_sel = jnp.where(validg[..., None], s_sel, -jnp.inf).reshape(B, H, G, top * MOBA_BLOCK)
        own = start // MOBA_BLOCK
        k_own = lax.dynamic_slice_in_dim(k_p, own * MOBA_BLOCK, MOBA_BLOCK, axis=2)
        v_own = lax.dynamic_slice_in_dim(v_p, own * MOBA_BLOCK, MOBA_BLOCK, axis=2)
        s_own = jnp.einsum('bhgd,bhkd->bhgk', qg, k_own).astype(jnp.float32) * scale
        qpos = start + jnp.arange(G)
        kpos = own * MOBA_BLOCK + jnp.arange(MOBA_BLOCK)
        s_own = jnp.where(kpos[None, :] <= qpos[:, None], s_own, -jnp.inf)
        p = jax.nn.softmax(jnp.concatenate([s_sel, s_own], axis=-1), axis=-1)
        p_sel = p[..., :top * MOBA_BLOCK].reshape(B, H, G, top, MOBA_BLOCK).astype(v.dtype)
        p_own = p[..., top * MOBA_BLOCK:].astype(v.dtype)
        return (jnp.einsum('bhgnk,bhgnkd->bhgd', p_sel, v_sel)
                + jnp.einsum('bhgk,bhkd->bhgd', p_own, v_own))

    out = lax.map(group, jnp.arange(s_pad // G))
    out = jnp.transpose(out, (1, 2, 0, 3, 4)).reshape(B, H, s_pad, dh)
    return out[:, :, :S]

def setup_inputs(seed: int = 0) -> dict:
    key = jax.random.key(seed)
    ks = jax.random.split(key, 16)
    f32 = jnp.float32
    nrm = lambda k, shape, fan: jax.random.normal(k, shape, f32) * (fan ** -0.5)
    gain = lambda k, shape: 1.0 + 0.02 * jax.random.normal(k, shape, f32)
    x = jax.random.normal(ks[0], (BATCH, SEQ, D_MODEL), f32)
    offsets = jax.random.randint(ks[1], (BATCH, 1), 0, 1024, dtype=jnp.int32)
    positions = (offsets + jnp.arange(SEQ, dtype=jnp.int32)[None, :]).astype(jnp.int32)
    return {
        "x": x,
        "positions": positions,
        "norm1_gain": gain(ks[2], (DEPTH, D_MODEL)),
        "w_in": nrm(ks[3], (DEPTH, D_MODEL, D_IN_PROJ), D_MODEL),
        "w_gate_up": nrm(ks[4], (DEPTH, GLA_GATE_RANK, GLA_QK), GLA_GATE_RANK),
        "b_gate": 0.1 * jax.random.normal(ks[5], (DEPTH, GLA_QK), f32),
        "gla_out_gain": gain(ks[6], (DEPTH, GLA_HEAD_V)),
        "moba_out_gain": gain(ks[7], (DEPTH, MOBA_HEAD_DIM)),
        "w_out": nrm(ks[8], (DEPTH, D_MIX, D_MODEL), D_MIX),
        "norm2_gain": gain(ks[9], (DEPTH, D_MODEL)),
        "w_ffn_gate": nrm(ks[10], (DEPTH, D_MODEL, D_FF), D_MODEL),
        "w_ffn_up": nrm(ks[11], (DEPTH, D_MODEL, D_FF), D_MODEL),
        "w_ffn_down": nrm(ks[12], (DEPTH, D_FF, D_MODEL), D_FF),
        "final_norm_gain": gain(ks[13], (D_MODEL,)),
    }

def reference(x, positions, norm1_gain, w_in, w_gate_up, b_gate, gla_out_gain, moba_out_gain,
              w_out, norm2_gain, w_ffn_gate, w_ffn_up, w_ffn_down, final_norm_gain):
    B, S, _ = x.shape
    dt = x.dtype
    to_heads = lambda t, h: t.reshape(B, S, h, -1).transpose(0, 2, 1, 3)
    for l in range(DEPTH):
        h = rms_norm(x, norm1_gain[l])
        proj = h @ w_in[l]
        parts = [proj[..., IN_OFFSETS[i]:IN_OFFSETS[i + 1]] for i in range(len(IN_SIZES))]
        gq, gk, gv, gr, g_low, mq, mk, mv = parts
        gate_logit = (g_low @ w_gate_up[l] + b_gate[l]).astype(jnp.float32)
        log_a = jax.nn.log_sigmoid(gate_logit) / GLA_GATE_TAU
        o_gla = gla_chunked(to_heads(gq, GLA_HEADS).astype(jnp.float32),
                            to_heads(gk, GLA_HEADS).astype(jnp.float32),
                            to_heads(gv, GLA_HEADS).astype(jnp.float32),
                            to_heads(log_a, GLA_HEADS)).astype(dt)
        o_gla = rms_norm(o_gla.transpose(0, 2, 1, 3), gla_out_gain[l])
        o_gla = (o_gla * jax.nn.silu(gr.reshape(B, S, GLA_HEADS, GLA_HEAD_V))).reshape(B, S, GLA_V)
        q_m = rotary(to_heads(mq, MOBA_HEADS), positions)
        k_m = rotary(to_heads(mk, MOBA_HEADS), positions)
        o_moba = moba_attention(q_m, k_m, to_heads(mv, MOBA_HEADS))
        o_moba = rms_norm(o_moba.transpose(0, 2, 1, 3), moba_out_gain[l]).reshape(B, S, MOBA_W)
        x = x + jnp.concatenate([o_gla, o_moba], axis=-1) @ w_out[l]
        h = rms_norm(x, norm2_gain[l])
        x = x + (jax.nn.silu(h @ w_ffn_gate[l]) * (h @ w_ffn_up[l])) @ w_ffn_down[l]
    return rms_norm(x, final_norm_gain)


_drawn_inputs = setup_inputs


def setup_inputs(seed=0):
    import zlib

    import numpy as np

    out = dict(_drawn_inputs(seed))
    spreads = {}
    factors = {'b_gate': 3.565,
     'gla_out_gain': 7.518,
     'moba_out_gain': 4.533,
     'norm2_gain': 4.757,
     'final_norm_gain': 2.75}
    for name, (base, spread) in spreads.items():
        noise = np.random.default_rng([zlib.crc32(name.encode()), seed]).standard_normal(out[name].shape)
        drawn = base * np.exp(spread * noise) if base else spread * noise
        out[name] = __import__('jax').numpy.asarray(drawn.astype(out[name].dtype))
    for name, factor in factors.items():
        out[name] = (out[name] * factor).astype(out[name].dtype)
    return out
```

```python
from contextlib import ExitStack

import numpy as np
import concourse.bass as bass
from concourse import mybir

P = 128
SEQ, D = 256, 1024
T = SEQ // P
KC = D // P
HEADS = 4
DV = 128
DK = 64
PAIRS = HEADS // 2
CHUNK = 64
CHUNKS = SEQ // CHUNK
RANK = 16
TAU = 16.0
QK = HEADS * DK
W = HEADS * DV
HALF = DV // 2
D_FF = 2816
EPS = 1e-6
ROPE_THETA = 10000.0
GQK, GV, GR, LOW, MQ, MK, MV = np.cumsum([0, 2 * QK, W, W, RANK, W, W]).tolist()
BLOCKS = (GQK, MQ, MK, MV, GV, GR)
FF = 256
PHASES = D_FF // FF
UNIT = 2048
RAW, RING = 3, 6
IN_UNITS, OUT_UNITS = 2 * len(BLOCKS), 4
PHASE0 = IN_UNITS + OUT_UNITS
UNITS = PHASE0 + 3 * PHASES
LOOPED = (PHASES - 3) // 2
SCALE = float(DV) ** -0.5
MASKED = -3.0e38
PI_BELOW = float(np.nextafter(np.float32(np.pi), np.float32(0)))
MAGIC = 1.5 * 2.0 ** 23
NORM1_ROW, NORM2_ROW, GLA_ROW, MOBA_ROW, GAIN_ROWS = 0, KC, 2 * KC, 2 * KC + 1, 2 * KC + 2
TWO_PI_BITS, TWO_PI_SCALE = 0x6487ED5110B4611A62633145C, 96


def two_pi_parts(n):
    rest, parts = TWO_PI_BITS, []
    for _ in range(n):
        grain = 1 << max(rest.bit_length() - 12, 0)
        part = rest // grain * grain
        parts.append(float(part) / 2.0 ** TWO_PI_SCALE)
        rest -= part
    return parts


def phase_unit(j):
    return PHASE0 + 3 * j - (1 if j else 0)


def build_block(nc, x, positions, norm1_gain, w_in, w_gate_up, b_gate, gla_out_gain, moba_out_gain,
                w_out, norm2_gain, w_ffn_gate, w_ffn_up, w_ffn_down, final_norm_gain, inv_freq, out):
    f32, f32r, i32 = mybir.dt.float32, mybir.dt.float32r, mybir.dt.int32
    ALU = mybir.AluOpType
    ACT = mybir.ActivationFunctionType
    AX = mybir.AxisListType

    with ExitStack() as ctx:
        def sb(name, shape, dt=f32):
            return ctx.enter_context(nc.sbuf_tensor(name, [P, *shape], dt))

        def sem(name):
            return ctx.enter_context(nc.semaphore(name))

        acc = ctx.enter_context(nc.psum_tensor("acc", [P, 4, 512], f32))
        aux = ctx.enter_context(nc.psum_tensor("aux", [P, 4, 512], f32))

        raw = sb("raw", [RAW, UNIT])
        w_hi = sb("w_hi", [RING, UNIT], f32r)
        w_lo = sb("w_lo", [RING, UNIT], f32r)
        x_sb = sb("x_sb", [T, D])
        aT_hi = sb("aT_hi", [KC, SEQ], f32r)
        aT_lo = sb("aT_lo", [KC, SEQ], f32r)
        pT_hi = sb("pT_hi", [2, SEQ], f32r)
        pT_lo = sb("pT_lo", [2, SEQ], f32r)
        low_hi = sb("low_hi", [KC, RANK], f32r)
        low_lo = sb("low_lo", [KC, RANK], f32r)

        ident = sb("ident", [P])
        tri_cum = sb("tri_cum", [P])
        tri_rest = sb("tri_rest", [P])
        chunk_ind = sb("chunk_ind", [2])
        gla_mask = sb("gla_mask", [P])
        causal = sb("causal", [2 * P])
        half_pi = sb("half_pi", [1])
        one = sb("one", [1])
        minus_half = sb("minus_half", [2 * HEADS])
        gains = sb("gains", [GAIN_ROWS])
        low_raw = sb("low_raw", [KC, RANK])
        w_up = sb("w_up", [QK])
        pos_i = sb("pos_i", [T], i32)
        pos_f = sb("pos_f", [T])
        freq = sb("freq", [HALF])
        cos_t = sb("cos_t", [T, HALF])
        sin_t = sb("sin_t", [T, HALF])
        ss = sb("ss", [3, T])
        ms = sb("ms", [3, T])
        rstd = sb("rstd", [3, T])
        ss_h = sb("ss_h", [2, 2 * HEADS])
        ms_h = sb("ms_h", [2, 2 * HEADS])
        l2_h = sb("l2_h", [2 * HEADS])
        rstd_h = sb("rstd_h", [2, 2 * HEADS])
        low = sb("low", [T, RANK])
        lowT = sb("lowT", [SEQ])
        qdT = sb("qdT", [PAIRS, 2, SEQ])
        kiT = sb("kiT", [PAIRS, SEQ])
        decay = sb("decay", [PAIRS, CHUNKS])
        state = sb("state", [CHUNKS - 1, PAIRS, DV])
        row_max = sb("row_max", [2 * HEADS])
        neg_max = sb("neg_max", [2 * HEADS])
        row_sum = sb("row_sum", [2 * HEADS])
        gv = sb("gv", [T, W])
        mv = sb("mv", [T, W])
        reuse_a = sb("reuse_a", [1024])
        reuse_b = sb("reuse_b", [1024])
        reuse_c = sb("reuse_c", [1536])
        reuse_d = sb("reuse_d", [1024])
        reuse_e = sb("reuse_e", [2048])
        reuse_f = sb("reuse_f", [2048])

        rot_tmp = mv[:, :, 0:HEADS * HALF].rearrange("p t (h d) -> p t h d", h=HEADS)
        turns_hi = w_lo[:, RING - 1, 0:P]
        gain_rows = reuse_d[:, 0:P]
        gain_f = reuse_a[:, :]
        gqk = reuse_a[:, :].rearrange("p (t n) -> p t n", t=T)
        o_gla = reuse_a[:, :].rearrange("p (t h v) -> p t h v", t=T, h=HEADS)
        soft = reuse_b[:, 0:512].rearrange("p (t n) -> p t n", t=T)
        log_a = reuse_b[:, 512:1024].rearrange("p (t n) -> p t n", t=T)
        a_gla = reuse_b[:, :].rearrange("p (t h s) -> p t h s", t=T, h=HEADS)
        q_dec, k_inv, k_end = (reuse_c[:, 512 * i:512 * i + 512].rearrange("p (t n) -> p t n", t=T)
                               for i in range(3))
        squares = reuse_c[:, 0:1024]
        silu_g = reuse_c[:, 0:512].rearrange("p (t n) -> p t n", t=T)
        hidden = reuse_c[:, 512:1024].rearrange("p (t n) -> p t n", t=T)
        m_raw = reuse_d[:, :].rearrange("p (t h d) -> p t h d", t=T, h=HEADS)
        o_moba = m_raw
        m_flat = reuse_d[:, :].rearrange("p (t n) -> p t n", t=T)
        m_rot = reuse_e[:, :].rearrange("p (w t h d) -> p w t h d", w=2, t=T, h=HEADS)
        s_0 = reuse_e[:, 0:512].rearrange("p (h k) -> p h k", h=HEADS)
        s_1 = reuse_e[:, 512:1536].rearrange("p (h k) -> p h k", h=HEADS)
        mT = reuse_f[:, :].rearrange("p (w h s) -> p w h s", w=2, h=HEADS)
        probT = reuse_f[:, 0:1536].rearrange("p (b h q) -> p b h q", b=3, h=HEADS)
        silu_r = reuse_f[:, 0:1024].rearrange("p (t h v) -> p t h v", t=T, h=HEADS)
        ang = reuse_e[:, 0:128]
        turns = reuse_e[:, 128:256]
        turns_lo = reuse_e[:, 256:384]
        sin_arg = reuse_e[:, 384:512]

        x_loaded = [sem(f"x_loaded_{t}") for t in range(T)]
        rows_loaded = sem("rows_loaded")
        low_loaded = sem("low_loaded")
        up_loaded = sem("up_loaded")
        pos_loaded = sem("pos_loaded")
        gain_f_loaded = sem("gain_f_loaded")
        raw_loaded = [sem(f"raw_loaded_{s}") for s in range(RAW)]
        out_stored = sem("out_stored")
        consts_built = sem("consts_built")
        ident_built = sem("ident_built")
        pool_seq = sem("pool_seq")
        act_seq = sem("act_seq")
        dve_seq = sem("dve_seq")
        gains_in_psum = sem("gains_in_psum")
        gains_ready = sem("gains_ready")
        xT_in_psum = sem("xT_in_psum")
        xT_hi_ready = sem("xT_hi_ready")
        xT_lo_ready = sem("xT_lo_ready")
        low_hi_ready = sem("low_hi_ready")
        low_lo_ready = sem("low_lo_ready")
        low_in_psum = sem("low_in_psum")
        low_ready = sem("low_ready")
        hi_ready = sem("hi_ready")
        lo_ready = sem("lo_ready")
        unit_used = sem("unit_used")
        ss_ready = sem("ss_ready")
        rstd_ready = sem("rstd_ready")
        rstd_h_ready = sem("rstd_h_ready")
        ms_h_ready = sem("ms_h_ready")
        angles_ready = sem("angles_ready")
        sin_ready = sem("sin_ready")
        tile0_in_psum = sem("tile0_in_psum")
        block_ready = sem("block_ready")
        rotated = sem("rotated")
        lowT_in_psum = sem("lowT_in_psum")
        lowT_ready = sem("lowT_ready")
        logits_in_psum = sem("logits_in_psum")
        soft_ready = sem("soft_ready")
        log_a_ready = sem("log_a_ready")
        cum_in_psum = sem("cum_in_psum")
        cum_exp_ready = sem("cum_exp_ready")
        gla_ops_ready = sem("gla_ops_ready")
        glaT_in_psum = sem("glaT_in_psum")
        glaT_by_act = sem("glaT_by_act")
        glaT_by_dve = sem("glaT_by_dve")
        mT_in_psum = sem("mT_in_psum")
        mT_by_act = sem("mT_by_act")
        mT_by_dve = sem("mT_by_dve")
        a_zeroed = sem("a_zeroed")
        a_in_psum = sem("a_in_psum")
        a_ready = sem("a_ready")
        scores_in_psum = sem("scores_in_psum")
        scores_taken = sem("scores_taken")
        max_ready = sem("max_ready")
        probs_ready = sem("probs_ready")
        probT_in_psum = sem("probT_in_psum")
        probT_by_act = sem("probT_by_act")
        probT_by_dve = sem("probT_by_dve")
        moba_in_psum = sem("moba_in_psum")
        update_in_psum = sem("update_in_psum")
        states_ready = sem("states_ready")
        gla_in_psum = sem("gla_in_psum")
        sq_ready = sem("sq_ready")
        silu_r_ready = sem("silu_r_ready")
        heads_ready = sem("heads_ready")
        headsT_in_psum = sem("headsT_in_psum")
        headsT_hi_ready = sem("headsT_hi_ready")
        headsT_lo_ready = sem("headsT_lo_ready")
        mixed_in_psum = sem("mixed_in_psum")
        x2_ready = sem("x2_ready")
        x2T_in_psum = sem("x2T_in_psum")
        x2T_hi_ready = sem("x2T_hi_ready")
        x2T_lo_ready = sem("x2T_lo_ready")
        gu_in_psum = sem("gu_in_psum")
        silu_ready = sem("silu_ready")
        hidden_ready = sem("hidden_ready")
        hiddenT_in_psum = sem("hiddenT_in_psum")
        hiddenT_hi_ready = sem("hiddenT_hi_ready")
        hiddenT_lo_ready = sem("hiddenT_lo_ready")
        down_in_psum = sem("down_in_psum")
        x3_ready = sem("x3_ready")
        out_ready = sem("out_ready")

        block = ctx.enter_context(nc.Block())

        @block.sync
        def _(sp):
            for t in range(T):
                sp.dma_start(x_sb[:, t, :], x[0, t * P:(t + 1) * P, :]).then_inc(x_loaded[t], 16)

            def load_unit(slot, parts):
                for dst, src in parts:
                    sp.dma_start(dst, src).then_inc(raw_loaded[slot], 16)

            def rows_unit(slot, w, row, n_rows, col, width):
                buf = raw[:, slot, :].rearrange("p (k n) -> p k n", k=n_rows)
                half = n_rows // 2
                load_unit(slot, [(buf[:, h * half:(h + 1) * half, :],
                                  w[row + h * half * P:row + (h + 1) * half * P, col:col + width]
                                  .rearrange("(k p) n -> p k n", p=P)) for h in range(2)])

            def gate_up_unit(slot, j, h):
                buf = raw[:, slot, :].rearrange("p (k w n) -> p k w n", k=4, w=2)
                rows = slice(4 * P * h, 4 * P * (h + 1))
                load_unit(slot, [(buf[:, :, g, :], w[0, rows, bass.ds(j * FF, FF)].rearrange("(k p) n -> p k n", p=P))
                                 for g, w in enumerate((w_ffn_gate, w_ffn_up))])

            def down_unit(slot, j):
                buf = raw[:, slot, :].rearrange("p (k n) -> p k n", k=2)
                load_unit(slot, [(buf[:, k, :], w_ffn_down[0, bass.ds(j * FF + k * P, P), :]) for k in range(2)])

            def raw_free(u):
                sp.wait_ge(lo_ready, u - (RAW - 1))

            for u in range(IN_UNITS):
                if u >= RAW:
                    raw_free(u)
                rows_unit(u % RAW, w_in[0], (u % 2) * 4 * P, 4, BLOCKS[u // 2], 512)
            for n in range(OUT_UNITS):
                u = IN_UNITS + n
                raw_free(u)
                rows_unit(u % RAW, w_out[0], ((n + 2) % 4) * 2 * P, 2, 0, D)

            def ffn_units(j, u, slot, with_down=True):
                for h in range(2):
                    raw_free(u + h)
                    gate_up_unit((slot + h) % RAW, j, h)
                if with_down:
                    raw_free(u + 2)
                    down_unit((slot + 2) % RAW, j - 1)

            ffn_units(0, PHASE0, PHASE0, with_down=False)
            ffn_units(1, phase_unit(1), phase_unit(1))
            sp.wait_ge(x2_ready, 2 * T)
            sp.dma_start(gain_f, final_norm_gain.unsqueeze(0).to_broadcast([P, D])).then_inc(gain_f_loaded, 16)
            with sp.Fori(0, LOOPED) as i:
                for a in range(2):
                    ffn_units(i * 2 + (2 + a), i * 6 + phase_unit(2 + a), phase_unit(2 + a))
            ffn_units(PHASES - 1, phase_unit(PHASES - 1), phase_unit(PHASES - 1))
            raw_free(UNITS - 1)
            down_unit((UNITS - 1) % RAW, PHASES - 1)

            for n in range(2 * T):
                t, half = n // 2, n % 2
                sp.wait_ge(out_ready, n + 1)
                cols = slice(half * 512, half * 512 + 512)
                sp.dma_start(out[0, t * P:(t + 1) * P, cols], x_sb[:, t, cols]).then_inc(out_stored, 16)
            sp.wait_ge(out_stored, 16 * 2 * T)

        @block.gpsimd
        def _(pool):
            n_seq = [0]

            def then(ins):
                n_seq[0] += 1
                ins.then_inc(pool_seq, 1)
                pool.wait_ge(pool_seq, n_seq[0])

            then(nc.gpsimd.memset(ident[:, :], 0.0))
            nc.gpsimd.affine_select(out=ident[:, :], in_=ident[:, :], compare_op=ALU.not_equal, fill=1.0, base=0,
                                    pattern=[[-1, P]], channel_multiplier=1).then_inc(ident_built, 1)
            nc.gpsimd.memset(half_pi[:, :], float(np.pi / 2))
            nc.gpsimd.memset(one[:, :], 1.0)
            nc.gpsimd.memset(lowT[:, :], 1.0)
            nc.gpsimd.memset(qdT[:, :, :, :], 0.0)
            nc.gpsimd.memset(tri_cum[:, :], 1.0 / TAU)
            nc.gpsimd.memset(tri_rest[:, :], 1.0 / TAU)
            nc.gpsimd.memset(gla_mask[:, :], 1.0)
            nc.gpsimd.memset(causal[:, :], 0.0)
            nc.gpsimd.memset(chunk_ind[:, :], 0.0)
            then(nc.gpsimd.memset(minus_half[:, :], -0.5))
            for tri, fill in ((tri_cum[:, :], 0.0), (gla_mask[:, :], 0.0)):
                nc.gpsimd.affine_select(out=tri, in_=tri, compare_op=ALU.is_ge, fill=fill, base=0,
                                        pattern=[[1, P]], channel_multiplier=-1)
            nc.gpsimd.affine_select(out=tri_rest[:, :], in_=tri_rest[:, :], compare_op=ALU.is_ge, fill=0.0, base=-1,
                                    pattern=[[-1, P]], channel_multiplier=1)
            diagonal = causal[:, P:2 * P]
            then(nc.gpsimd.affine_select(out=diagonal, in_=diagonal, compare_op=ALU.is_ge, fill=MASKED, base=0,
                                         pattern=[[-1, P]], channel_multiplier=1))
            nc.gpsimd.memset(tri_cum[0:CHUNK, CHUNK:P], 0.0)
            nc.gpsimd.memset(gla_mask[0:CHUNK, CHUNK:P], 0.0)
            nc.gpsimd.memset(tri_rest[CHUNK:P, 0:CHUNK], 0.0)
            nc.gpsimd.memset(chunk_ind[0:CHUNK, 0:1], 1.0 / TAU)
            nc.gpsimd.memset(chunk_ind[CHUNK:P, 1:2], 1.0 / TAU).then_inc(consts_built, 1)
            pool.wait_ge(consts_built, 1)

            def wide_rstd(norm, t):
                pool.wait_ge(ss_ready, norm * T + t + 1)
                then(nc.gpsimd.tensor_scalar(ms[:, norm, t:t + 1], ss[:, norm, t:t + 1], 1.0 / D, EPS, ALU.mult, ALU.add))
                nc.gpsimd.tensor_tensor(rstd[:, norm, t:t + 1], ms[:, norm, t:t + 1], minus_half[:, 0:1],
                                        ALU.pow).then_inc(rstd_ready, 1)

            for t in range(T):
                wide_rstd(0, t)
            pool.wait_ge(cum_in_psum, 1)
            nc.gpsimd.memset(reuse_b[:, :], 0.0).then_inc(a_zeroed, 1)
            for group in range(2):
                pool.wait_ge(ms_h_ready, group + 1)
                nc.gpsimd.tensor_tensor(rstd_h[:, group, :], ms_h[:, group, :], minus_half[:, :],
                                        ALU.pow).then_inc(rstd_h_ready, 1)
            for norm in (1, 2):
                for t in range(T):
                    wide_rstd(norm, t)

        @block.tensor
        def _(pe):
            def product(dst, k, t, right_hi, right_lo, first, last, left_hi=aT_hi, left_lo=aT_lo):
                tok = slice(t * P, (t + 1) * P)
                nc.tensor.matmul(dst, left_hi[:, k, tok], right_hi, start=first, stop=False)
                nc.tensor.matmul(dst, left_hi[:, k, tok], right_lo, start=False, stop=False)
                return nc.tensor.matmul(dst, left_lo[:, k, tok], right_hi, start=False, stop=last)

            def unit_ready(n):
                pe.wait_ge(hi_ready, n)
                pe.wait_ge(lo_ready, n)

            def weights(slot, width, k, lo=0, hi=None):
                hi = width if hi is None else hi
                return (w_hi[:, slot, k * width + lo:k * width + hi], w_lo[:, slot, k * width + lo:k * width + hi])

            pe.wait_ge(ident_built, 1)
            pe.wait_ge(rows_loaded, 64)
            nc.tensor.transpose(acc[:, 3, 0:GAIN_ROWS], gain_rows[0:GAIN_ROWS, :],
                                ident[0:GAIN_ROWS, 0:GAIN_ROWS]).then_inc(gains_in_psum, 1)
            for t in range(T):
                pe.wait_ge(x_loaded[t], 16)
            for bank in range(4):
                for k in (2 * bank, 2 * bank + 1):
                    for t in range(T):
                        last = nc.tensor.transpose(aux[:, bank, (k % 2) * SEQ + t * P:(k % 2) * SEQ + (t + 1) * P],
                                                   x_sb[:, t, k * P:(k + 1) * P], ident[:, :])
                last.then_inc(xT_in_psum, 1)

            pe.wait_ge(low_hi_ready, 1)
            pe.wait_ge(low_lo_ready, 1)
            pe.wait_ge(xT_hi_ready, KC)
            pe.wait_ge(xT_lo_ready, KC)
            for t in range(T):
                for k in range(KC):
                    last = product(acc[:, 2, t * RANK:(t + 1) * RANK], k, t, low_hi[:, k, :], low_lo[:, k, :],
                                   k == 0, k == KC - 1)
            last.then_inc(low_in_psum, 1)

            def in_unit(u):
                b, h = u // 2, u % 2
                unit_ready(u + 1)
                if b == 1 and h == 0:
                    pe.wait_ge(low_ready, 1)
                    pe.wait_ge(gains_ready, 1)
                if b >= 2 and h == 0:
                    pe.wait_ge(block_ready, 2 * (b - 1))
                for t in range(T):
                    for k in range(4):
                        last = product(acc[:, 2 * (b % 2) + t, :], 4 * h + k, t, *weights(u % RING, 512, k),
                                       h == 0 and k == 0, h == 1 and k == 3)
                    if h == 1 and t == 0:
                        last.then_inc(tile0_in_psum, 1)
                last.then_inc(unit_used, 1)

            def transposes(bank, blocks):
                for n, src in enumerate(blocks):
                    last = nc.tensor.transpose(aux[:, bank, n * P:(n + 1) * P], src, ident[:, :])
                return last

            def low_transposed():
                pe.wait_ge(low_ready, 1)
                for t in range(T):
                    last = nc.tensor.transpose(aux[0:RANK, 0, t * P:(t + 1) * P], low[:, t, :], ident[:, :])
                last.then_inc(lowT_in_psum, 1)

            def logits():
                pe.wait_ge(lowT_ready, 1)
                pe.wait_ge(up_loaded, 32)
                for t in range(T):
                    last = nc.tensor.matmul(aux[:, 1, t * QK:(t + 1) * QK], lowT[0:RANK + 1, t * P:(t + 1) * P],
                                            w_up[0:RANK + 1, :], start=True, stop=True)
                last.then_inc(logits_in_psum, 1)

            def cumulate():
                pe.wait_ge(log_a_ready, 1)
                pe.wait_ge(consts_built, 1)
                for t in range(T):
                    nc.tensor.matmul(aux[:, 2, t * QK:(t + 1) * QK], tri_cum[:, :], log_a[:, t, :], start=True, stop=True)
                    nc.tensor.matmul(aux[:, 3, t * QK:(t + 1) * QK], tri_rest[:, :], log_a[:, t, :], start=True, stop=True)
                    for pair in range(PAIRS):
                        c = pair * CHUNKS + 2 * t
                        last = nc.tensor.matmul(aux[:, 0, c:c + 2], log_a[:, t, pair * P:(pair + 1) * P],
                                                chunk_ind[:, :], start=True, stop=True)
                last.then_inc(cum_in_psum, 1)

            def gla_transposed():
                pe.wait_ge(gla_ops_ready, 2)
                for bank, src in ((1, q_dec), (2, k_inv)):
                    transposes(bank, [src[:, t, pair * P:(pair + 1) * P] for pair in range(PAIRS)
                                      for t in range(T)]).then_inc(glaT_in_psum, 1)

            def moba_transposed(which, banks):
                pe.wait_ge(rotated, which + 1)
                if which == 1:
                    pe.wait_ge(glaT_by_act, 2)
                    pe.wait_ge(glaT_by_dve, 1)
                for n, bank in enumerate(banks):
                    transposes(bank, [m_rot[:, which, t, h, :] for h in (2 * n, 2 * n + 1)
                                      for t in range(T)]).then_inc(mT_in_psum, 1)

            def gla_scores():
                pe.wait_ge(mT_by_act, 1)
                pe.wait_ge(mT_by_dve, 1)
                for t, bank in ((0, 3), (1, 0)):
                    tok = slice(t * P, (t + 1) * P)
                    for pair in range(PAIRS):
                        last = nc.tensor.matmul(aux[:, bank, pair * SEQ:(pair + 1) * SEQ], kiT[:, pair, tok],
                                                qdT[:, pair, :, tok], start=True, stop=True)
                    last.then_inc(a_in_psum, 1)

            def moba_scores():
                pe.wait_ge(mT_by_act, 2)
                pe.wait_ge(mT_by_dve, 2)
                for h in range(HEADS):
                    last = nc.tensor.matmul(aux[:, 1, h * P:(h + 1) * P], mT[:, 0, h, 0:P], mT[:, 1, h, 0:P],
                                            start=True, stop=True)
                last.then_inc(scores_in_psum, 1)
                for h in range(HEADS):
                    if h == 2:
                        pe.wait_ge(a_ready, 1)
                    last = nc.tensor.matmul(aux[:, 2 + h // 2, (h % 2) * SEQ:(h % 2 + 1) * SEQ], mT[:, 0, h, P:SEQ],
                                            mT[:, 1, h, :], start=True, stop=True)
                    if h % 2:
                        last.then_inc(scores_in_psum, 1)

            def probs_transposed():
                pe.wait_ge(probs_ready, 1)
                pe.wait_ge(a_ready, 2)
                for bank, (s, k) in enumerate(((s_0, 0), (s_1, 0), (s_1, P))):
                    transposes(bank, [s[:, h, k:k + P] for h in range(HEADS)]).then_inc(probT_in_psum, 1)

            def moba_outputs():
                pe.wait_ge(probT_by_act, 2)
                pe.wait_ge(probT_by_dve, 1)
                pe.wait_ge(block_ready, 8)
                for t, bank in ((0, 3), (1, 0)):
                    for h in range(HEADS):
                        for k in range(t + 1):
                            last = nc.tensor.matmul(aux[:, bank, h * DV:(h + 1) * DV], probT[:, t + k, h, :],
                                                    mv[:, k, h * DV:(h + 1) * DV], start=k == 0, stop=k == t)
                    last.then_inc(moba_in_psum, 1)

            def gla_updates():
                pe.wait_ge(block_ready, 10)
                pe.wait_ge(gla_ops_ready, 3)
                for c in range(CHUNKS - 1):
                    t, rows = c // 2, slice((c % 2) * CHUNK, (c % 2 + 1) * CHUNK)
                    for h in range(HEADS):
                        pair, half = h // 2, slice((h % 2) * DK, (h % 2 + 1) * DK)
                        col = (c // 2) * PAIRS * DV + pair * DV
                        last = nc.tensor.matmul(aux[half, 1 + c % 2, col:col + DV],
                                                k_end[rows, t, h * DK:(h + 1) * DK], gv[rows, t, h * DV:(h + 1) * DV],
                                                start=True, stop=True)
                last.then_inc(update_in_psum, 1)

            def gla_outputs():
                pe.wait_ge(a_ready, 2)
                pe.wait_ge(states_ready, 1)
                for t in range(T):
                    for h in range(HEADS):
                        pair, par = h // 2, h % 2
                        cols = slice(h * DV, (h + 1) * DV)
                        nc.tensor.matmul(aux[:, 1 + t, cols], a_gla[:, t, h, :], gv[:, t, cols], start=True, stop=True)
                        for c in range(max(2 * t, 1), 2 * t + 2):
                            rows = slice((c % 2) * CHUNK, (c % 2 + 1) * CHUNK)
                            last = nc.tensor.matmul(aux[rows, 1 + t, cols],
                                                    qdT[:, pair, par, c * CHUNK:(c + 1) * CHUNK],
                                                    state[:, c - 1, pair, :], start=False, stop=True,
                                                    skip_group_check=True)
                    last.then_inc(gla_in_psum, 1)

            def heads_transposed(group, banks):
                for t, bank in enumerate(banks):
                    n = 2 * group + t
                    pe.wait_ge(heads_ready, n + 1)
                    o = (o_moba, o_gla)[group]
                    transposes(bank, [o[:, t, h, :] for h in range(HEADS)]).then_inc(headsT_in_psum, 1)

            def out_product(t, group, n):
                for k in range(4):
                    u = IN_UNITS + 2 * group + k // 2
                    last = product(acc[:, 2 * t + n, :], (KC // 2, 0)[group] + k, t,
                                   *weights(u % RING, D, k % 2, 512 * n, 512 * n + 512),
                                   group == 0 and k == 0, group == 1 and k == 3)
                    if t == 1 and n == 1 and k % 2:
                        last.then_inc(unit_used, 1)
                if group == 1 and not (t == 1 and n == 1):
                    last.then_inc(mixed_in_psum, 1)

            def x2_transposed(t, banks):
                for n, bank in enumerate(banks):
                    pe.wait_ge(x2_ready, 2 * t + n + 1)
                    transposes(bank, [x_sb[:, t, k * P:(k + 1) * P] for k in range(4 * n, 4 * n + 4)]).then_inc(x2T_in_psum, 1)

            def gate_up(slot, h, t):
                for k in range(4):
                    last = product(aux[:, 3 * t, :], 4 * h + k, t, *weights(slot, 512, k),
                                   h == 0 and k == 0, h == 1 and k == 3)
                if t == 1:
                    last.then_inc(unit_used, 1)
                elif h == 1:
                    last.then_inc(gu_in_psum, 1)

            def hidden_transposed(j, free=True):
                pe.wait_ge(hidden_ready, j * 2)
                if free:
                    pe.wait_ge(hiddenT_hi_ready, j - 1)
                    pe.wait_ge(hiddenT_lo_ready, j - 1)
                transposes(1, [hidden[:, t, k * P:(k + 1) * P] for k in range(2)
                               for t in range(T)]).then_inc(hiddenT_in_psum, 1)

            def down(slot, j, first=False, last_phase=False):
                pe.wait_ge(hiddenT_hi_ready, j)
                pe.wait_ge(hiddenT_lo_ready, j)
                for t in range(T):
                    for n in range(2):
                        for k in range(2):
                            last = product(acc[:, 2 * t + n, :], k, t, *weights(slot, D, k, 512 * n, 512 * n + 512),
                                           first and k == 0, last_phase and k == 1, pT_hi, pT_lo)
                        if last_phase:
                            last.then_inc(down_in_psum, 1)
                if not last_phase:
                    last.then_inc(unit_used, 1)

            def ffn_phase(j, u, slot, first=False):
                hidden_transposed(j, free=not first)
                for h in range(2):
                    unit_ready(u + (h + 1))
                    for t in range(T):
                        gate_up((slot + h) % RING, h, t)
                unit_ready(u + 3)
                down((slot + 2) % RING, j, first)

            between = {1: [low_transposed], 2: [logits], 3: [cumulate], 5: [gla_transposed],
                       6: [lambda: moba_transposed(0, (3, 0))],
                       7: [lambda: moba_transposed(1, (1, 2)), gla_scores], 8: [moba_scores],
                       9: [probs_transposed], 10: [moba_outputs, gla_updates],
                       11: [lambda: heads_transposed(0, (3, 0)), gla_outputs]}
            for u in range(IN_UNITS):
                in_unit(u)
                for step in between.get(u, ()):
                    step()

            for t in range(T):
                pe.wait_ge(headsT_hi_ready, t + 1)
                pe.wait_ge(headsT_lo_ready, t + 1)
                pe.wait_ge(block_ready, 10) if t == 0 else pe.wait_ge(silu_r_ready, 2)
                for n in range(2):
                    if t == 0 and n == 0:
                        unit_ready(IN_UNITS + 2)
                    out_product(t, 0, n)
            heads_transposed(1, (1, 2))
            unit_ready(IN_UNITS + 4)
            for t in range(T):
                pe.wait_ge(headsT_hi_ready, 2 + t + 1)
                pe.wait_ge(headsT_lo_ready, 2 + t + 1)
                for n in range(2):
                    out_product(t, 1, n)
                    if t == 1 and n == 0:
                        x2_transposed(0, (0, 3))

            for t in range(T):
                pe.wait_ge(x2T_hi_ready, (t + 1) * KC)
                pe.wait_ge(x2T_lo_ready, (t + 1) * KC)
                for h in range(2):
                    unit_ready(PHASE0 + h + 1)
                    gate_up((PHASE0 + h) % RING, h, t)
                    if t == 0 and h == 0:
                        x2_transposed(1, (1, 2))

            ffn_phase(1, phase_unit(1), phase_unit(1) % RING, first=True)
            with pe.Fori(0, LOOPED) as i:
                for a in range(2):
                    ffn_phase(i * 2 + (2 + a), i * 6 + phase_unit(2 + a), phase_unit(2 + a) % RING)
            ffn_phase(PHASES - 1, phase_unit(PHASES - 1), phase_unit(PHASES - 1) % RING)
            hidden_transposed(PHASES)
            unit_ready(UNITS)
            down((UNITS - 1) % RING, PHASES, last_phase=True)

        @block.scalar
        def _(act):
            n_seq = [0]

            def then(ins):
                n_seq[0] += 1
                ins.then_inc(act_seq, 1)
                act.wait_ge(act_seq, n_seq[0])

            for row, n_rows, src in ((NORM1_ROW, KC, norm1_gain.rearrange("l (k p) -> (l k) p", p=P)),
                                     (NORM2_ROW, KC, norm2_gain.rearrange("l (k p) -> (l k) p", p=P)),
                                     (GLA_ROW, 1, gla_out_gain), (MOBA_ROW, 1, moba_out_gain)):
                act.dma_start(gain_rows[row:row + n_rows, :], src).then_inc(rows_loaded, 16)
            act.dma_start(low_raw[:, :, :], w_in[0, :, LOW:LOW + RANK].rearrange("(k p) n -> p k n", p=P)).then_inc(low_loaded, 16)
            act.dma_start(w_up[0:RANK, :], w_gate_up[0]).then_inc(up_loaded, 16)
            act.dma_start(w_up[RANK:RANK + 1, :], b_gate).then_inc(up_loaded, 16)
            with nc.allow_non_contiguous_dma(reason="256 positions, one per partition and tile"):
                act.dma_start(pos_i[:, :], positions.rearrange("b (t p) -> p (b t)", p=P)).then_inc(pos_loaded, 16)
            act.dma_start(freq[:, :], inv_freq.to_broadcast([P, HALF])).then_inc(pos_loaded, 16)

            def split_as(slot, fill, used=None):
                act.wait_ge(raw_loaded[slot % RAW], fill * 32)
                if used is not None:
                    act.wait_ge(unit_used, used)
                nc.scalar.copy(w_hi[:, slot % RING, :], raw[:, slot % RAW, :]).then_inc(hi_ready, 1)

            def split(u):
                split_as(u, u // RAW + 1, u - RING + 1 if u >= RING else None)

            def sum_squares(norm, t, junk):
                nc.scalar.activation(junk, x_sb[:, t, :], ACT.Square, accum_out=ss[:, norm, t:t + 1]).then_inc(ss_ready, 1)

            def take_block(b, dst):
                for t in range(T):
                    if t == 0:
                        act.wait_ge(tile0_in_psum, b + 1)
                    else:
                        act.wait_ge(unit_used, 2 * b + 2)
                    act.wait_ge(rstd_ready, t + 1)
                    nc.scalar.activation(dst[:, t], acc[:, 2 * (b % 2) + t, :], ACT.Copy,
                                         scale=rstd[:, 0, t:t + 1]).then_inc(block_ready, 1)

            act.wait_ge(gains_ready, 1)
            for k in range(KC):
                act.wait_ge(xT_in_psum, k // 2 + 1)
                nc.scalar.mul(aT_hi[:, k, :], aux[:, k // 2, (k % 2) * SEQ:(k % 2 + 1) * SEQ],
                              gains[:, NORM1_ROW + k:NORM1_ROW + k + 1]).then_inc(xT_hi_ready, 1)
            act.wait_ge(low_loaded, 16)
            nc.scalar.copy(low_hi[:, :, :], low_raw[:, :, :]).then_inc(low_hi_ready, 1)
            split(0)
            split(1)
            for t, junk in enumerate((reuse_c[:, 0:D], reuse_f[:, 0:D])):
                act.wait_ge(x_loaded[t], 16)
                sum_squares(0, t, junk)
            split(2)
            act.wait_ge(angles_ready, 1)
            act.wait_ge(consts_built, 1)
            nc.scalar.activation(sin_t[:, :, :], ang.rearrange("p (t d) -> p t d", t=T), ACT.Sin)
            nc.scalar.activation(cos_t[:, :, :], sin_arg.rearrange("p (t d) -> p t d", t=T), ACT.Sin,
                                 bias=half_pi[:, :], scale=-1.0).then_inc(sin_ready, 1)
            split(3)
            take_block(0, gqk)
            split(4)
            act.wait_ge(logits_in_psum, 1)
            flat = reuse_b[:, 0:512]
            then(nc.scalar.activation(flat, aux[:, 1, :], ACT.Abs))
            then(nc.scalar.activation(flat, flat, ACT.Exp, scale=-1.0))
            nc.scalar.activation(flat, flat, ACT.Ln, bias=one[:, :]).then_inc(soft_ready, 1)
            split(5)
            take_block(1, m_flat)
            act.wait_ge(cum_in_psum, 1)
            nc.scalar.activation(reuse_c[:, 0:512], aux[:, 2, :], ACT.Exp)
            nc.scalar.activation(reuse_c[:, 512:1024], aux[:, 2, :], ACT.Exp, scale=-1.0)
            nc.scalar.activation(reuse_c[:, 1024:1536], aux[:, 3, :], ACT.Exp)
            nc.scalar.activation(decay[:, :, :], aux[:, 0, 0:PAIRS * CHUNKS].rearrange("p (a c) -> p a c", a=PAIRS),
                                 ACT.Exp).then_inc(cum_exp_ready, 1)
            split(6)
            split(7)
            act.wait_ge(rotated, 1)
            take_block(2, m_flat)
            act.wait_ge(glaT_in_psum, 1)
            nc.scalar.copy(qdT[0:DK, :, 0, :], aux[0:DK, 1, :].rearrange("p (a s) -> p a s", a=PAIRS)).then_inc(glaT_by_act, 1)
            act.wait_ge(glaT_in_psum, 2)
            nc.scalar.copy(kiT[:, :, :], aux[:, 2, :].rearrange("p (a s) -> p a s", a=PAIRS)).then_inc(glaT_by_act, 1)
            split(8)
            act.wait_ge(mT_in_psum, 1)
            nc.scalar.copy(mT[:, 0, 0:2, :], aux[:, 3, :].rearrange("p (h s) -> p h s", h=2)).then_inc(mT_by_act, 1)
            split(9)
            act.wait_ge(rotated, 2)
            take_block(3, mv)
            act.wait_ge(mT_in_psum, 3)
            nc.scalar.copy(mT[:, 1, 0:2, :], aux[:, 1, :].rearrange("p (h s) -> p h s", h=2)).then_inc(mT_by_act, 1)
            split(10)
            split(11)
            act.wait_ge(max_ready, 1)
            for t, s in ((0, s_0), (1, s_1)):
                for h in range(HEADS):
                    c = t * HEADS + h
                    last = nc.scalar.activation(s[:, h, :], s[:, h, :], ACT.Exp, bias=neg_max[:, c:c + 1], scale=SCALE,
                                                accum_out=row_sum[:, c:c + 1])
            last.then_inc(probs_ready, 1)
            take_block(4, gv)
            split(12)
            for b in range(2):
                act.wait_ge(probT_in_psum, b + 1)
                nc.scalar.copy(probT[:, b, :, :], aux[:, b, :].rearrange("p (h q) -> p h q", h=HEADS)).then_inc(probT_by_act, 1)
            split(13)
            for t, bank in ((0, 3), (1, 0)):
                act.wait_ge(moba_in_psum, t + 1)
                nc.scalar.activation(squares[:, t * W:(t + 1) * W], aux[:, bank, :], ACT.Square).then_inc(sq_ready, 1)
            split(14)
            split(15)
            for t in range(T):
                if t == 0:
                    act.wait_ge(tile0_in_psum, len(BLOCKS))
                else:
                    act.wait_ge(unit_used, IN_UNITS)
                nc.scalar.activation(silu_r[:, t, :, :], acc[:, 2 + t, :].rearrange("p (h v) -> p h v", h=HEADS), ACT.Silu,
                                     scale=rstd[:, 0, t:t + 1]).then_inc(silu_r_ready, 1)

            def take_headsT(group, banks):
                row = (MOBA_ROW, GLA_ROW)[group]
                base = (HEADS, 0)[group]
                for t, bank in enumerate(banks):
                    act.wait_ge(headsT_in_psum, 2 * group + t + 1)
                    nc.scalar.mul(aT_hi[:, base:base + HEADS, t * P:(t + 1) * P],
                                  aux[:, bank, :].rearrange("p (h q) -> p h q", h=HEADS),
                                  gains[:, row:row + 1]).then_inc(headsT_hi_ready, 1)

            act.wait_ge(ms_h_ready, 1)
            take_headsT(0, (3, 0))
            for t in range(T):
                act.wait_ge(gla_in_psum, t + 1)
                nc.scalar.activation(squares[:, t * W:(t + 1) * W], aux[:, 1 + t, :], ACT.Square).then_inc(sq_ready, 1)
            split(16)
            split(17)
            take_headsT(1, (1, 2))

            def take_x2T(t, banks):
                for k in range(KC):
                    act.wait_ge(x2T_in_psum, 2 * t + k // 4 + 1)
                    nc.scalar.mul(aT_hi[:, k, t * P:(t + 1) * P], aux[:, banks[k // 4], (k % 4) * P:(k % 4 + 1) * P],
                                  gains[:, NORM2_ROW + k:NORM2_ROW + k + 1]).then_inc(x2T_hi_ready, 1)

            def take_gate(j, u):
                for t in range(T):
                    if t == 0:
                        act.wait_ge(gu_in_psum, j + 1)
                    else:
                        act.wait_ge(unit_used, u + 2)
                    if isinstance(j, int):
                        act.wait_ge(rstd_ready, T + t + 1)
                    nc.scalar.activation(silu_g[:, t, :], aux[:, 3 * t, 0:FF], ACT.Silu,
                                         scale=rstd[:, 1, t:t + 1]).then_inc(silu_ready, 1)

            act.wait_ge(x2_ready, 2)
            sum_squares(1, 0, reuse_f[:, 0:D])
            take_x2T(0, (0, 3))
            split(18)
            split(19)
            act.wait_ge(x2_ready, 4)
            sum_squares(1, 1, reuse_e[:, 0:D])
            take_x2T(1, (1, 2))
            split(20)
            take_gate(0, PHASE0)

            def ffn_phase(j, u, fill, slot, n_units=3):
                act.wait_ge(hiddenT_in_psum, j)
                act.wait_ge(unit_used, u)
                nc.scalar.copy(pT_hi[:, :, :], aux[:, 1, :].rearrange("p (k s) -> p k s", k=2)).then_inc(hiddenT_hi_ready, 1)
                for n in range(n_units):
                    split_as(slot + 3 + n, fill, u + (n + 4 - RING))
                take_gate(j, u)

            ffn_phase(1, phase_unit(1), phase_unit(2) // RAW + 1, phase_unit(1))
            with act.Fori(0, LOOPED) as i:
                for a in range(2):
                    ffn_phase(i * 2 + (2 + a), i * 6 + phase_unit(2 + a), i * 2 + (phase_unit(3 + a) // RAW + 1), phase_unit(2 + a))
            ffn_phase(PHASES - 1, phase_unit(PHASES - 1), phase_unit(PHASES) // RAW + 1, phase_unit(PHASES - 1), n_units=1)
            act.wait_ge(hiddenT_in_psum, PHASES)
            act.wait_ge(unit_used, UNITS - 1)
            nc.scalar.copy(pT_hi[:, :, :], aux[:, 1, :].rearrange("p (k s) -> p k s", k=2)).then_inc(hiddenT_hi_ready, 1)
            for t, junk in enumerate((reuse_f[:, 0:D], reuse_e[:, 0:D])):
                act.wait_ge(x3_ready, 2 * t + 2)
                sum_squares(2, t, junk)

        @block.vector
        def _(dve):
            n_seq = [0]

            def then(ins):
                n_seq[0] += 1
                ins.then_inc(dve_seq, 1)
                dve.wait_ge(dve_seq, n_seq[0])

            def split(u, slot=None):
                slot = u if slot is None else slot
                dve.wait_ge(hi_ready, u + 1)
                nc.vector.tensor_tensor(w_lo[:, slot % RING, :], raw[:, slot % RAW, :],
                                        w_hi[:, slot % RING, :].bitcast(f32), ALU.subtract).then_inc(lo_ready, 1)

            def lo_of_scaled(out_lo, src, gain, hi):
                return nc.vector.scalar_tensor_tensor(out=out_lo, in0=src, scalar=gain, in1=hi.bitcast(f32),
                                                      op0=ALU.mult, op1=ALU.subtract)

            dve.wait_ge(gains_in_psum, 1)
            nc.vector.tensor_copy(gains[:, :], acc[:, 3, 0:GAIN_ROWS]).then_inc(gains_ready, 1)
            dve.wait_ge(gains_ready, 1)
            for k in range(KC):
                dve.wait_ge(xT_hi_ready, k // 2 * 2 + 2)
                lo_of_scaled(aT_lo[:, k, :], aux[:, k // 2, (k % 2) * SEQ:(k % 2 + 1) * SEQ],
                             gains[:, NORM1_ROW + k:NORM1_ROW + k + 1], aT_hi[:, k, :]).then_inc(xT_lo_ready, 1)
            dve.wait_ge(low_hi_ready, 1)
            nc.vector.tensor_tensor(low_lo[:, :, :], low_raw[:, :, :], low_hi[:, :, :].bitcast(f32),
                                    ALU.subtract).then_inc(low_lo_ready, 1)
            split(0)
            split(1)

            dve.wait_ge(pos_loaded, 32)
            then(nc.vector.tensor_copy(pos_f[:, :], pos_i[:, :]))
            for t in range(T):
                last = nc.vector.tensor_scalar(ang[:, t * HALF:(t + 1) * HALF], freq[:, :], pos_f[:, t:t + 1], None, ALU.mult)
            then(last)

            def nearest_turns():
                then(nc.vector.tensor_scalar(turns, ang, 1.0 / (2.0 * np.pi), MAGIC, ALU.mult, ALU.add))
                then(nc.vector.tensor_scalar(turns, turns, -MAGIC, None, ALU.add))

            def take_off(n, part):
                then(nc.vector.scalar_tensor_tensor(out=ang, in0=n, scalar=-part, in1=ang, op0=ALU.mult, op1=ALU.add))

            nearest_turns()
            then(nc.vector.tensor_copy(turns_hi, turns))
            then(nc.vector.tensor_tensor(turns_lo, turns, turns_hi.bitcast(f32), ALU.subtract))
            for part in two_pi_parts(5):
                take_off(turns_hi.bitcast(f32), part)
                take_off(turns_lo, part)
            nearest_turns()
            for part in two_pi_parts(3):
                take_off(turns, part)
            then(nc.vector.tensor_scalar(ang, ang, PI_BELOW, -PI_BELOW, ALU.min, ALU.max))
            nc.vector.scalar_tensor_tensor(out=sin_arg, in0=ang, scalar=-1.0, in1=ang, op0=ALU.mult, op1=ALU.max).then_inc(angles_ready, 1)

            split(2)
            dve.wait_ge(low_in_psum, 1)
            dve.wait_ge(rstd_ready, T)
            for t in range(T):
                last = nc.vector.tensor_scalar(low[:, t, :], acc[:, 2, t * RANK:(t + 1) * RANK], rstd[:, 0, t:t + 1],
                                               None, ALU.mult)
            last.then_inc(low_ready, 1)
            split(3)
            dve.wait_ge(lowT_in_psum, 1)
            dve.wait_ge(consts_built, 1)
            nc.vector.tensor_copy(lowT[0:RANK, :], aux[0:RANK, 0, 0:SEQ]).then_inc(lowT_ready, 1)
            split(4)
            dve.wait_ge(soft_ready, 1)
            nc.vector.scalar_tensor_tensor(out=reuse_b[:, 512:1024], in0=aux[:, 1, :], scalar=0.0, in1=reuse_b[:, 0:512],
                                           op0=ALU.min, op1=ALU.subtract).then_inc(log_a_ready, 1)
            split(5)

            def rotate(which):
                dve.wait_ge(block_ready, 4 + 2 * which)
                dve.wait_ge(sin_ready, 1)
                cos, sin = (v[:, :, :].unsqueeze(2).to_broadcast([P, T, HEADS, HALF]) for v in (cos_t, sin_t))
                a, b = m_raw[:, :, :, 0:HALF], m_raw[:, :, :, HALF:DV]
                out_a, out_b = m_rot[:, which, :, :, 0:HALF], m_rot[:, which, :, :, HALF:DV]
                nc.vector.tensor_tensor(out_a, a, cos, ALU.mult)
                nc.vector.tensor_tensor(out_b, b, cos, ALU.mult)
                then(nc.vector.tensor_tensor(rot_tmp, b, sin, ALU.mult))
                then(nc.vector.tensor_tensor(out_a, out_a, rot_tmp, ALU.subtract))
                then(nc.vector.tensor_tensor(rot_tmp, a, sin, ALU.mult))
                nc.vector.tensor_tensor(out_b, out_b, rot_tmp, ALU.add).then_inc(rotated, 1)

            rotate(0)
            split(6)
            dve.wait_ge(cum_exp_ready, 1)
            nc.vector.scalar_tensor_tensor(out=q_dec, in0=gqk[:, :, 0:QK], scalar=float(DK) ** -0.5, in1=q_dec,
                                           op0=ALU.mult, op1=ALU.mult).then_inc(gla_ops_ready, 1)
            nc.vector.tensor_tensor(k_inv, gqk[:, :, QK:2 * QK], k_inv, ALU.mult).then_inc(gla_ops_ready, 1)
            nc.vector.tensor_tensor(k_end, gqk[:, :, QK:2 * QK], k_end, ALU.mult).then_inc(gla_ops_ready, 1)
            split(7)
            rotate(1)
            dve.wait_ge(glaT_in_psum, 1)
            nc.vector.tensor_copy(qdT[DK:P, :, 1, :], aux[DK:P, 1, :].rearrange("p (a s) -> p a s", a=PAIRS)).then_inc(glaT_by_dve, 1)
            split(8)
            dve.wait_ge(mT_in_psum, 2)
            nc.vector.tensor_copy(mT[:, 0, 2:4, :], aux[:, 0, :].rearrange("p (h s) -> p h s", h=2)).then_inc(mT_by_dve, 1)
            split(9)
            dve.wait_ge(mT_in_psum, 4)
            nc.vector.tensor_copy(mT[:, 1, 2:4, :], aux[:, 2, :].rearrange("p (h s) -> p h s", h=2)).then_inc(mT_by_dve, 1)
            dve.wait_ge(a_zeroed, 1)
            mask = gla_mask[:, :].bitcast(i32).unsqueeze(1).to_broadcast([P, HEADS, P])
            for t, bank in ((0, 3), (1, 0)):
                dve.wait_ge(a_in_psum, t + 1)
                nc.vector.copy_predicated(a_gla[:, t, :, :], mask,
                                          aux[:, bank, :].rearrange("p (h s) -> p h s", h=HEADS)).then_inc(a_ready, 1)
            split(10)
            dve.wait_ge(scores_in_psum, 1)
            nc.vector.tensor_tensor(s_0, aux[:, 1, :].rearrange("p (h k) -> p h k", h=HEADS),
                                    causal[:, P:2 * P].unsqueeze(1).to_broadcast([P, HEADS, P]), ALU.add)
            for n in range(2):
                dve.wait_ge(scores_in_psum, n + 2)
                last = nc.vector.tensor_tensor(s_1[:, 2 * n:2 * n + 2, :], aux[:, 2 + n, :].rearrange("p (h k) -> p h k", h=2),
                                               causal[:, :].unsqueeze(1).to_broadcast([P, 2, 2 * P]), ALU.add)
            then(last)
            nc.vector.reduce_max(row_max[:, 0:HEADS], s_0, AX.X)
            then(nc.vector.reduce_max(row_max[:, HEADS:2 * HEADS], s_1, AX.X))
            nc.vector.tensor_scalar(neg_max[:, :], row_max[:, :], -SCALE, None, ALU.mult).then_inc(max_ready, 1)
            split(11)
            split(12)
            dve.wait_ge(probT_in_psum, 3)
            nc.vector.tensor_copy(probT[:, 2, :, :], aux[:, 2, :].rearrange("p (h q) -> p h q", h=HEADS)).then_inc(probT_by_dve, 1)
            split(13)
            dve.wait_ge(update_in_psum, 1)

            def update(c):
                col = (c // 2) * PAIRS * DV
                return aux[:, 1 + c % 2, col:col + PAIRS * DV].rearrange("p (a v) -> p a v", a=PAIRS)

            then(nc.vector.tensor_copy(state[:, 0, :, :], update(0)))
            for c in range(1, CHUNKS - 1):
                for pair in range(PAIRS):
                    last = nc.vector.scalar_tensor_tensor(out=state[:, c, pair, :], in0=state[:, c - 1, pair, :],
                                                          scalar=decay[:, pair, c:c + 1], in1=update(c)[:, pair, :],
                                                          op0=ALU.mult, op1=ALU.add)
                    if c < CHUNKS - 2:
                        then(last)
            last.then_inc(states_ready, 1)

            def head_squares(group):
                dve.wait_ge(sq_ready, 2 * group + 2)
                then(nc.vector.reduce_sum(ss_h[:, group, :], squares.rearrange("p (c v) -> p c v", v=DV), AX.X))

            head_squares(0)
            then(nc.vector.scalar_tensor_tensor(out=l2_h[:, :], in0=row_sum[:, :], scalar=EPS, in1=row_sum[:, :],
                                                op0=ALU.mult, op1=ALU.mult))
            nc.vector.scalar_tensor_tensor(out=ms_h[:, 0, :], in0=ss_h[:, 0, :], scalar=1.0 / DV, in1=l2_h[:, :],
                                           op0=ALU.mult, op1=ALU.add).then_inc(ms_h_ready, 1)

            def normed(group, t, bank, dst):
                factor = rstd_h[:, group, t * HEADS:(t + 1) * HEADS].unsqueeze(2).to_broadcast([P, HEADS, DV])
                return nc.vector.tensor_tensor(dst, aux[:, bank, :].rearrange("p (h v) -> p h v", h=HEADS), factor, ALU.mult)

            split(14)
            dve.wait_ge(rstd_h_ready, 1)
            for t, bank in ((0, 3), (1, 0)):
                normed(0, t, bank, o_moba[:, t, :, :]).then_inc(heads_ready, 1)
            split(15)

            def take_headsT(group, banks):
                row = (MOBA_ROW, GLA_ROW)[group]
                base = (HEADS, 0)[group]
                for t, bank in enumerate(banks):
                    dve.wait_ge(headsT_hi_ready, 2 * group + t + 1)
                    dst = slice(base, base + HEADS), slice(t * P, (t + 1) * P)
                    lo_of_scaled(aT_lo[:, dst[0], dst[1]], aux[:, bank, :].rearrange("p (h q) -> p h q", h=HEADS),
                                 gains[:, row:row + 1], aT_hi[:, dst[0], dst[1]]).then_inc(headsT_lo_ready, 1)

            take_headsT(0, (3, 0))
            head_squares(1)
            nc.vector.tensor_scalar(ms_h[:, 1, :], ss_h[:, 1, :], 1.0 / DV, EPS, ALU.mult, ALU.add).then_inc(ms_h_ready, 1)
            dve.wait_ge(rstd_h_ready, 2)
            dve.wait_ge(silu_r_ready, 2)
            normed(1, 0, 1, o_gla[:, 0, :, :])
            then(normed(1, 1, 2, o_gla[:, 1, :, :]))
            for t in range(T):
                nc.vector.tensor_tensor(o_gla[:, t, :, :], o_gla[:, t, :, :], silu_r[:, t, :, :], ALU.mult).then_inc(heads_ready, 1)
            split(16)
            split(17)
            take_headsT(1, (1, 2))

            def residual(t, n, ready):
                cols = slice(512 * n, 512 * n + 512)
                nc.vector.tensor_tensor(x_sb[:, t, cols], acc[:, 2 * t + n, :], x_sb[:, t, cols], ALU.add).then_inc(ready, 1)

            def take_x2T(t, banks):
                for k in range(KC):
                    dve.wait_ge(x2T_hi_ready, t * KC + k // 4 * 4 + 4)
                    tok = slice(t * P, (t + 1) * P)
                    lo_of_scaled(aT_lo[:, k, tok], aux[:, banks[k // 4], (k % 4) * P:(k % 4 + 1) * P],
                                 gains[:, NORM2_ROW + k:NORM2_ROW + k + 1], aT_hi[:, k, tok]).then_inc(x2T_lo_ready, 1)

            for n in range(2):
                dve.wait_ge(mixed_in_psum, n + 1)
                residual(0, n, x2_ready)
            dve.wait_ge(mixed_in_psum, 3)
            residual(1, 0, x2_ready)
            take_x2T(0, (0, 3))
            dve.wait_ge(unit_used, PHASE0)
            residual(1, 1, x2_ready)
            split(18)
            split(19)
            take_x2T(1, (1, 2))
            split(20)

            def take_up(j):
                for t in range(T):
                    dve.wait_ge(silu_ready, j * 2 + (t + 1))
                    nc.vector.scalar_tensor_tensor(out=hidden[:, t, :], in0=aux[:, 3 * t, FF:2 * FF], scalar=rstd[:, 1, t:t + 1],
                                                   in1=silu_g[:, t, :], op0=ALU.mult, op1=ALU.mult).then_inc(hidden_ready, 1)

            def take_hiddenT(j):
                dve.wait_ge(hiddenT_hi_ready, j)
                nc.vector.tensor_tensor(pT_lo[:, :, :], aux[:, 1, :].rearrange("p (k s) -> p k s", k=2),
                                        pT_hi[:, :, :].bitcast(f32), ALU.subtract).then_inc(hiddenT_lo_ready, 1)

            def ffn_phase(j, u, slot, n_units=3):
                take_hiddenT(j)
                for n in range(n_units):
                    split(u + 3 + n, slot + 3 + n)
                take_up(j)

            take_up(0)
            ffn_phase(1, phase_unit(1), phase_unit(1))
            with dve.Fori(0, LOOPED) as i:
                for a in range(2):
                    ffn_phase(i * 2 + (2 + a), i * 6 + phase_unit(2 + a), phase_unit(2 + a))
            ffn_phase(PHASES - 1, phase_unit(PHASES - 1), phase_unit(PHASES - 1), n_units=1)
            take_hiddenT(PHASES)

            for n in range(2 * T):
                dve.wait_ge(down_in_psum, n + 1)
                residual(n // 2, n % 2, x3_ready)
            dve.wait_ge(gain_f_loaded, 16)
            dve.wait_ge(x3_ready, 2 * T)
            for n in range(2 * T):
                t, cols = n // 2, slice((n % 2) * 512, (n % 2 + 1) * 512)
                dve.wait_ge(rstd_ready, 2 * T + t + 1)
                nc.vector.scalar_tensor_tensor(out=x_sb[:, t, cols], in0=x_sb[:, t, cols], scalar=rstd[:, 2, t:t + 1],
                                               in1=gain_f[:, cols], op0=ALU.mult, op1=ALU.mult).then_inc(out_ready, 1)


_INS = ["x", "positions", "norm1_gain", "w_in", "w_gate_up", "b_gate", "gla_out_gain", "moba_out_gain", "w_out",
        "norm2_gain", "w_ffn_gate", "w_ffn_up", "w_ffn_down", "final_norm_gain"]


def kernel(**inputs):
    import numpy as _np
    import concourse.bacc as _bacc
    from concourse import mybir as _mybir
    from concourse.bass_utils import run_bass_kernel_spmd as _run

    nc = _bacc.Bacc("TRN2", target_bir_lowering=False, num_devices=1)
    arrays = {name: _np.ascontiguousarray(inputs[name]) for name in _INS}
    arrays["inv_freq"] = _np.power(_np.float32(ROPE_THETA), -_np.arange(HALF, dtype=_np.float32) / HALF)[None].astype(_np.float32)
    args = [nc.dram_tensor(f"in_{name}", a.shape, _mybir.dt.from_np(a.dtype), kind="ExternalInput").ap()
            for name, a in arrays.items()]
    out = nc.dram_tensor("out", (1, SEQ, D), _mybir.dt.float32, kind="ExternalOutput").ap()
    build_block(nc, *args, out)
    r = _run(nc, [{f"in_{name}": a for name, a in arrays.items()}], core_ids=[0])
    return r.results[0]["out"]
```

```python
from contextlib import ExitStack

import numpy as np
import concourse.bass as bass
from concourse import mybir

P = 128
SEQ, D = 256, 1024
T = SEQ // P
KC = D // P
HEADS = 4
DV = 128
DK = 64
PAIRS = HEADS // 2
CHUNK = 64
CHUNKS = SEQ // CHUNK
RANK = 16
TAU = 16.0
QK = HEADS * DK
W = HEADS * DV
HALF = DV // 2
D_FF = 2816
EPS = 1e-6
ROPE_THETA = 10000.0
GQK, GV, GR, LOW, MQ, MK, MV = np.cumsum([0, 2 * QK, W, W, RANK, W, W]).tolist()
BLOCKS = (GQK, MQ, MK, MV, GV, GR)
FF = 256
PHASES = D_FF // FF
UNIT = 2048
RAW, RING = 3, 6
IN_UNITS, OUT_UNITS = 2 * len(BLOCKS), 4
PHASE0 = IN_UNITS + OUT_UNITS
UNITS = PHASE0 + 3 * PHASES
LOOPED = (PHASES - 3) // 2
LOW_COPIES = [P, KC, P // (2 * RANK), RANK]
SCALE = float(DV) ** -0.5
GATE_UP_BANKS = ((0, 3), (2, 3))
X2T_BANKS = (0, 3, 1, 2)
MASKED = -3.0e38
PI_BELOW = float(np.nextafter(np.float32(np.pi), np.float32(0)))
MAGIC = 1.5 * 2.0 ** 23
NORM1_ROW, NORM2_ROW, GLA_ROW, MOBA_ROW, GAIN_ROWS = 0, KC, 2 * KC, 2 * KC + 1, 2 * KC + 2
TWO_PI_BITS, TWO_PI_SCALE = 0x6487ED5110B4611A62633145C, 96


def two_pi_parts(n):
    rest, parts = TWO_PI_BITS, []
    for _ in range(n):
        grain = 1 << max(rest.bit_length() - 12, 0)
        part = rest // grain * grain
        parts.append(float(part) / 2.0 ** TWO_PI_SCALE)
        rest -= part
    return parts


def phase_unit(j):
    return PHASE0 + 3 * j - (1 if j else 0)


def fill(u):
    return u // RAW + (1 if u % RAW else 0)


def build_block(nc, x, positions, norm1_gain, w_in, w_gate_up, b_gate, gla_out_gain, moba_out_gain,
                w_out, norm2_gain, w_ffn_gate, w_ffn_up, w_ffn_down, final_norm_gain, inv_freq, out):
    f32, f32r, i32 = mybir.dt.float32, mybir.dt.float32r, mybir.dt.int32
    ALU = mybir.AluOpType
    ACT = mybir.ActivationFunctionType
    AX = mybir.AxisListType

    with ExitStack() as ctx:
        def sb(name, shape, dt=f32):
            return ctx.enter_context(nc.sbuf_tensor(name, [P, *shape], dt))

        def sem(name):
            return ctx.enter_context(nc.semaphore(name))

        acc = ctx.enter_context(nc.psum_tensor("acc", [P, 4, 512], f32))
        aux = ctx.enter_context(nc.psum_tensor("aux", [P, 4, 512], f32))

        raw = sb("raw", [RAW, UNIT])
        w_hi = sb("w_hi", [RING, UNIT], f32r)
        w_lo = sb("w_lo", [RING, UNIT], f32r)
        x_sb = sb("x_sb", [T, D])
        aT_hi = sb("aT_hi", [KC, SEQ], f32r)
        aT_lo = sb("aT_lo", [KC, SEQ], f32r)
        pT_hi = sb("pT_hi", [2, SEQ], f32r)
        pT_lo = sb("pT_lo", [2, SEQ], f32r)

        ident = sb("ident", [P])
        tri_cum = sb("tri_cum", [P])
        tri_rest = sb("tri_rest", [P])
        chunk_ind = sb("chunk_ind", [2])
        gla_mask = sb("gla_mask", [P])
        causal = sb("causal", [2 * P])
        half_pi = sb("half_pi", [1])
        one = sb("one", [1])
        minus_half = sb("minus_half", [2 * HEADS])
        gains = sb("gains", [GAIN_ROWS])
        low_raw = sb("low_raw", [KC, RANK])
        w_up = sb("w_up", [QK])
        pos_i = sb("pos_i", [T], i32)
        pos_f = sb("pos_f", [T])
        freq = sb("freq", [HALF])
        cos_t = sb("cos_t", [T, HALF])
        sin_t = sb("sin_t", [T, HALF])
        ss = sb("ss", [2, T])
        ss_f = sb("ss_f", [T, 2])
        ms = sb("ms", [3, T])
        rstd = sb("rstd", [3, T])
        ss_h = sb("ss_h", [2, 2 * HEADS])
        ms_h = sb("ms_h", [2, 2 * HEADS])
        l2_h = sb("l2_h", [2 * HEADS])
        rstd_h = sb("rstd_h", [2, 2 * HEADS])
        lowT = sb("lowT", [SEQ])
        qdT = sb("qdT", [PAIRS, 2, SEQ])
        kiT = sb("kiT", [PAIRS, SEQ])
        decay = sb("decay", [PAIRS, CHUNKS])
        state = sb("state", [CHUNKS - 1, PAIRS, DV])
        row_max = sb("row_max", [2 * HEADS])
        neg_max = sb("neg_max", [2 * HEADS])
        row_sum = sb("row_sum", [2 * HEADS])
        gv = sb("gv", [T, W])
        mv = sb("mv", [T, W])
        reuse_a = sb("reuse_a", [1024])
        reuse_b = sb("reuse_b", [1024])
        reuse_c = sb("reuse_c", [1536])
        reuse_d = sb("reuse_d", [1024])
        reuse_e = sb("reuse_e", [2048])
        reuse_f = sb("reuse_f", [2048])

        gate_bias = mv[:, 0, W - QK:W]
        rot_tmp = mv[:, :, 0:HEADS * HALF].rearrange("p t (h d) -> p t h d", h=HEADS)
        low_w = w_hi[:, RING - 1, 0:KC * P].rearrange("p (k r w n) -> p k r w n", k=KC, w=2, n=RANK)
        turns_hi = w_lo[:, RING - 1, 0:P]
        gain_rows = reuse_d[:, 0:P]
        other_rows = reuse_d[:, P:2 * P]
        gain_f = reuse_a[:, :]
        gqk = reuse_a[:, :].rearrange("p (t n) -> p t n", t=T)
        o_gla = reuse_a[:, :].rearrange("p (t h v) -> p t h v", t=T, h=HEADS)
        soft = reuse_b[:, 0:512].rearrange("p (t n) -> p t n", t=T)
        log_a = reuse_b[:, 512:1024].rearrange("p (t n) -> p t n", t=T)
        a_gla = reuse_b[:, :].rearrange("p (t h s) -> p t h s", t=T, h=HEADS)
        q_dec, k_inv, k_end = (reuse_c[:, 512 * i:512 * i + 512].rearrange("p (t n) -> p t n", t=T)
                               for i in range(3))
        squares = reuse_c[:, 0:1024]
        silu_g = reuse_c[:, 0:512].rearrange("p (t n) -> p t n", t=T)
        hidden = reuse_c[:, 512:1024].rearrange("p (t n) -> p t n", t=T)
        out_sb = reuse_e[:, :].rearrange("p (t n) -> p t n", t=T)
        m_raw = reuse_d[:, :].rearrange("p (t h d) -> p t h d", t=T, h=HEADS)
        o_moba = m_raw
        m_flat = reuse_d[:, :].rearrange("p (t n) -> p t n", t=T)
        m_rot = reuse_e[:, :].rearrange("p (w t h d) -> p w t h d", w=2, t=T, h=HEADS)
        s_0 = reuse_e[:, 0:512].rearrange("p (h k) -> p h k", h=HEADS)
        s_1 = reuse_e[:, 512:1536].rearrange("p (h k) -> p h k", h=HEADS)
        mT = reuse_f[:, :].rearrange("p (w h s) -> p w h s", w=2, h=HEADS)
        probT = reuse_f[:, 0:1536].rearrange("p (b h q) -> p b h q", b=3, h=HEADS)
        silu_r = reuse_f[:, 0:1024].rearrange("p (t h v) -> p t h v", t=T, h=HEADS)
        ang, turns, turns_lo, sin_arg = (reuse_e[:, n * T * HALF:(n + 1) * T * HALF] for n in range(4))

        x_loaded = [sem(f"x_loaded_{t}") for t in range(T)]
        rows_loaded = sem("rows_loaded")
        norm1_loaded = sem("norm1_loaded")
        low_loaded = sem("low_loaded")
        bias_loaded = sem("bias_loaded")
        first_loaded = [sem(f"first_loaded_{n}") for n in range(2)]
        up_loaded = sem("up_loaded")
        pos_loaded = sem("pos_loaded")
        gain_f_loaded = sem("gain_f_loaded")
        raw_loaded = [sem(f"raw_loaded_{s}") for s in range(RAW)]
        out_stored = sem("out_stored")
        consts_built = sem("consts_built")
        ident_built = sem("ident_built")
        pool_seq = sem("pool_seq")
        act_seq = sem("act_seq")
        dve_seq = sem("dve_seq")
        gains_in_psum = sem("gains_in_psum")
        gains_ready = sem("gains_ready")
        xT_in_psum = sem("xT_in_psum")
        xT_hi_ready = sem("xT_hi_ready")
        xT_lo_ready = sem("xT_lo_ready")
        first_hi_ready = sem("first_hi_ready")
        first_lo_ready = sem("first_lo_ready")
        low_hi_ready = sem("low_hi_ready")
        low_lo_ready = sem("low_lo_ready")
        low_in_psum = sem("low_in_psum")
        hi_ready = sem("hi_ready")
        lo_ready = sem("lo_ready")
        unit_used = sem("unit_used")
        ss_ready = sem("ss_ready")
        rstd_ready = sem("rstd_ready")
        rstd_h_ready = sem("rstd_h_ready")
        ms_h_ready = sem("ms_h_ready")
        angles_ready = sem("angles_ready")
        sin_ready = sem("sin_ready")
        tile0_in_psum = sem("tile0_in_psum")
        block_ready = sem("block_ready")
        rotated = sem("rotated")
        lowT_ready = sem("lowT_ready")
        logits_in_psum = sem("logits_in_psum")
        logits_ready = sem("logits_ready")
        soft_ready = sem("soft_ready")
        log_a_ready = sem("log_a_ready")
        cum_in_psum = sem("cum_in_psum")
        cum_exp_ready = sem("cum_exp_ready")
        gla_ops_ready = sem("gla_ops_ready")
        glaT_in_psum = sem("glaT_in_psum")
        glaT_by_act = sem("glaT_by_act")
        glaT_by_dve = sem("glaT_by_dve")
        mT_in_psum = sem("mT_in_psum")
        mT_by_act = sem("mT_by_act")
        mT_by_dve = sem("mT_by_dve")
        a_zeroed = sem("a_zeroed")
        a_in_psum = sem("a_in_psum")
        a_ready = sem("a_ready")
        scores_in_psum = sem("scores_in_psum")
        max_ready = sem("max_ready")
        probs_ready = sem("probs_ready")
        probT_in_psum = sem("probT_in_psum")
        probT_by_act = sem("probT_by_act")
        probT_by_dve = sem("probT_by_dve")
        moba_in_psum = sem("moba_in_psum")
        update_in_psum = sem("update_in_psum")
        states_ready = sem("states_ready")
        gla_in_psum = sem("gla_in_psum")
        sq_ready = sem("sq_ready")
        silu_r_ready = sem("silu_r_ready")
        heads_ready = sem("heads_ready")
        headsT_in_psum = sem("headsT_in_psum")
        headsT_hi_ready = sem("headsT_hi_ready")
        headsT_lo_ready = sem("headsT_lo_ready")
        mixed_in_psum = sem("mixed_in_psum")
        x2_ready = sem("x2_ready")
        x2T_in_psum = sem("x2T_in_psum")
        x2T_hi_ready = sem("x2T_hi_ready")
        x2T_lo_ready = sem("x2T_lo_ready")
        gu_in_psum = sem("gu_in_psum")
        silu_ready = sem("silu_ready")
        hidden_ready = sem("hidden_ready")
        hiddenT_in_psum = sem("hiddenT_in_psum")
        hiddenT_hi_ready = sem("hiddenT_hi_ready")
        hiddenT_lo_ready = sem("hiddenT_lo_ready")
        down_in_psum = sem("down_in_psum")
        x3_ready = sem("x3_ready")
        x3_sums_ready = sem("x3_sums_ready")
        gained = sem("gained")
        out_left_ready = sem("out_left_ready")
        out_right_ready = sem("out_right_ready")

        block = ctx.enter_context(nc.Block())

        @block.sync
        def _(sp):
            for t in range(T):
                sp.dma_start(x_sb[:, t, :], x[0, t * P:(t + 1) * P, :]).then_inc(x_loaded[t], 16)

            def load_unit(slot, parts):
                for dst, src in parts:
                    sp.dma_start(dst, src).then_inc(raw_loaded[slot], 16)

            def rows_unit(slot, w, row, n_rows, col, width):
                buf = raw[:, slot, :].rearrange("p (k n) -> p k n", k=n_rows)
                half = n_rows // 2
                load_unit(slot, [(buf[:, h * half:(h + 1) * half, :],
                                  w[row + h * half * P:row + (h + 1) * half * P, col:col + width]
                                  .rearrange("(k p) n -> p k n", p=P)) for h in range(2)])

            def gate_up_unit(slot, j, h):
                buf = raw[:, slot, :].rearrange("p (k w n) -> p k w n", k=4, w=2)
                rows = slice(4 * P * h, 4 * P * (h + 1))
                load_unit(slot, [(buf[:, :, g, :], w[0, rows, bass.ds(j * FF, FF)].rearrange("(k p) n -> p k n", p=P))
                                 for g, w in enumerate((w_ffn_gate, w_ffn_up))])

            def down_unit(slot, j):
                buf = raw[:, slot, :].rearrange("p (k n) -> p k n", k=2)
                load_unit(slot, [(buf[:, k, :], w_ffn_down[0, bass.ds(j * FF + k * P, P), :]) for k in range(2)])

            def raw_free(u):
                if isinstance(u, int) and u == RAW:
                    sp.wait_ge(first_lo_ready, 4)
                else:
                    sp.wait_ge(lo_ready, u - RAW)

            buf = raw[:, 0, :].rearrange("p (k n) -> p k n", k=4)
            for h in range(2):
                sp.dma_start(buf[:, 2 * h:2 * h + 2, :], w_in[0, 2 * h * P:2 * (h + 1) * P, BLOCKS[0]:BLOCKS[0] + 512]
                             .rearrange("(k p) n -> p k n", p=P)).then_inc(first_loaded[h], 16)
            sp.dma_start(low_raw[:, :, :], w_in[0, :, LOW:LOW + RANK].rearrange("(k p) n -> p k n", p=P)).then_inc(low_loaded, 16)
            for u in range(1, RAW):
                rows_unit(u, w_in[0], (u % 2) * 4 * P, 4, BLOCKS[u // 2], 512)
            for row, n_rows, src in ((NORM2_ROW, KC, norm2_gain.rearrange("l (k p) -> (l k) p", p=P)),
                                     (GLA_ROW, 1, gla_out_gain), (MOBA_ROW, 1, moba_out_gain)):
                sp.dma_start(other_rows[row - KC:row - KC + n_rows, :], src).then_inc(rows_loaded, 16)
            for n in range(2):
                sp.dma_start(w_up[n * RANK:(n + 1) * RANK, :], w_gate_up[0]).then_inc(up_loaded, 16)
            sp.dma_start(gate_bias, b_gate.to_broadcast([P, QK])).then_inc(bias_loaded, 16)
            for u in range(RAW, IN_UNITS):
                raw_free(u)
                rows_unit(u % RAW, w_in[0], (u % 2) * 4 * P, 4, BLOCKS[u // 2], 512)
            for n in range(OUT_UNITS):
                u = IN_UNITS + n
                raw_free(u)
                rows_unit(u % RAW, w_out[0], ((n + 2) % 4) * 2 * P, 2, 0, D)

            def ffn_units(j, u, slot, with_down=True):
                for h in range(2):
                    raw_free(u + h)
                    gate_up_unit((slot + h) % RAW, j, h)
                if with_down:
                    raw_free(u + 2)
                    down_unit((slot + 2) % RAW, j - 1)

            ffn_units(0, PHASE0, PHASE0, with_down=False)
            ffn_units(1, phase_unit(1), phase_unit(1))
            sp.wait_ge(x2_ready, 2 * T)
            sp.dma_start(gain_f, final_norm_gain.unsqueeze(0).to_broadcast([P, D])).then_inc(gain_f_loaded, 16)
            with sp.Fori(0, LOOPED) as i:
                for a in range(2):
                    ffn_units(i * 2 + (2 + a), i * 6 + phase_unit(2 + a), phase_unit(2 + a))
            ffn_units(PHASES - 1, phase_unit(PHASES - 1), phase_unit(PHASES - 1))
            raw_free(UNITS - 1)
            down_unit((UNITS - 1) % RAW, PHASES - 1)

            for t in range(T):
                halves = ((out_left_ready, slice(0, 512)), (out_right_ready, slice(512, D)))
                for ready, cols in (halves if t else halves[::-1]):
                    sp.wait_ge(ready, t + 1)
                    sp.dma_start(out[0, t * P:(t + 1) * P, cols], out_sb[:, t, cols]).then_inc(out_stored, 16)
            sp.wait_ge(out_stored, 16 * 2 * T)

        @block.gpsimd
        def _(pool):
            n_seq = [0]

            def then(ins):
                n_seq[0] += 1
                ins.then_inc(pool_seq, 1)
                pool.wait_ge(pool_seq, n_seq[0])

            with nc.allow_non_contiguous_dma(reason="256 positions, one per partition and tile"):
                pool.dma_start(pos_i[:, :], positions.rearrange("b (t p) -> p (b t)", p=P)).then_inc(pos_loaded, 16)
            pool.dma_start(freq[:, :], inv_freq.to_broadcast([P, HALF])).then_inc(pos_loaded, 16)
            then(nc.gpsimd.memset(ident[:, :], 0.0))
            nc.gpsimd.affine_select(out=ident[:, :], in_=ident[:, :], compare_op=ALU.not_equal, fill=1.0, base=0,
                                    pattern=[[-1, P]], channel_multiplier=1).then_inc(ident_built, 1)
            nc.gpsimd.memset(half_pi[:, :], float(np.pi / 2))
            nc.gpsimd.memset(one[:, :], 1.0)
            nc.gpsimd.memset(qdT[:, :, :, :], 0.0)
            nc.gpsimd.memset(tri_cum[:, :], 1.0 / TAU)
            nc.gpsimd.memset(tri_rest[:, :], 1.0 / TAU)
            nc.gpsimd.memset(gla_mask[:, :], 1.0)
            nc.gpsimd.memset(causal[:, :], 0.0)
            nc.gpsimd.memset(chunk_ind[:, :], 0.0)
            then(nc.gpsimd.memset(minus_half[:, :], -0.5))
            for tri in (tri_cum[:, :], gla_mask[:, :]):
                nc.gpsimd.affine_select(out=tri, in_=tri, compare_op=ALU.is_ge, fill=0.0, base=0,
                                        pattern=[[1, P]], channel_multiplier=-1)
            nc.gpsimd.affine_select(out=tri_rest[:, :], in_=tri_rest[:, :], compare_op=ALU.is_ge, fill=0.0, base=-1,
                                    pattern=[[-1, P]], channel_multiplier=1)
            diagonal = causal[:, P:2 * P]
            then(nc.gpsimd.affine_select(out=diagonal, in_=diagonal, compare_op=ALU.is_ge, fill=MASKED, base=0,
                                         pattern=[[-1, P]], channel_multiplier=1))
            nc.gpsimd.memset(tri_cum[0:CHUNK, CHUNK:P], 0.0)
            nc.gpsimd.memset(gla_mask[0:CHUNK, CHUNK:P], 0.0)
            nc.gpsimd.memset(tri_rest[CHUNK:P, 0:CHUNK], 0.0)
            nc.gpsimd.memset(chunk_ind[0:CHUNK, 0:1], 1.0 / TAU)
            nc.gpsimd.memset(chunk_ind[CHUNK:P, 1:2], 1.0 / TAU).then_inc(consts_built, 1)
            pool.wait_ge(consts_built, 1)

            def wide_rstd(norm, t):
                pool.wait_ge(ss_ready, norm * T + t + 1)
                then(nc.gpsimd.tensor_scalar(ms[:, norm, t:t + 1], ss[:, norm, t:t + 1], 1.0 / D, EPS, ALU.mult, ALU.add))
                nc.gpsimd.tensor_tensor(rstd[:, norm, t:t + 1], ms[:, norm, t:t + 1], minus_half[:, 0:1],
                                        ALU.pow).then_inc(rstd_ready, 1)

            pool.wait_ge(low_hi_ready, 1)
            nc.gpsimd.tensor_tensor(low_w[:, :, :, 1, :], low_raw[:, :, :].unsqueeze(2).to_broadcast(LOW_COPIES),
                                    low_w[:, :, :, 0, :].bitcast(f32), ALU.subtract).then_inc(low_lo_ready, 1)
            for t in range(T):
                wide_rstd(0, t)
            pool.wait_ge(cum_in_psum, 1)
            nc.gpsimd.memset(reuse_b[:, :], 0.0).then_inc(a_zeroed, 1)
            for group in range(2):
                pool.wait_ge(ms_h_ready, group + 1)
                nc.gpsimd.tensor_tensor(rstd_h[:, group, :], ms_h[:, group, :], minus_half[:, :],
                                        ALU.pow).then_inc(rstd_h_ready, 1)
            for t in range(T):
                wide_rstd(1, t)
            for t in range(T):
                pool.wait_ge(x3_sums_ready, 2 * t + 1)
                then(nc.gpsimd.tensor_scalar(ms[:, 2, t:t + 1], ss_f[:, t, 0:1], 1.0 / D, EPS, ALU.mult, ALU.add))
                pool.wait_ge(x3_sums_ready, 2 * t + 2)
                then(nc.gpsimd.tensor_scalar(ss_f[:, t, 1:2], ss_f[:, t, 1:2], 1.0 / D, ms[:, 2, t:t + 1], ALU.mult, ALU.add))
                nc.gpsimd.tensor_tensor(rstd[:, 2, t:t + 1], ss_f[:, t, 1:2], minus_half[:, 0:1],
                                        ALU.pow).then_inc(rstd_ready, 1)

        @block.tensor
        def _(pe):
            def product(dst, k, t, right_hi, right_lo, first, last, left_hi=aT_hi, left_lo=aT_lo):
                tok = slice(t * P, (t + 1) * P)
                nc.tensor.matmul(dst, left_hi[:, k, tok], right_hi, start=first, stop=False)
                nc.tensor.matmul(dst, left_hi[:, k, tok], right_lo, start=False, stop=False)
                return nc.tensor.matmul(dst, left_lo[:, k, tok], right_hi, start=False, stop=last)

            def unit_ready(u):
                pe.wait_ge(hi_ready, u)
                pe.wait_ge(lo_ready, u)

            def weights(slot, width, k, lo=0, hi=None):
                hi = width if hi is None else hi
                return (w_hi[:, slot, k * width + lo:k * width + hi], w_lo[:, slot, k * width + lo:k * width + hi])

            pe.wait_ge(ident_built, 1)
            pe.wait_ge(norm1_loaded, 16)
            nc.tensor.transpose(acc[:, 3, NORM1_ROW:NORM1_ROW + KC], gain_rows[0:KC, :],
                                ident[0:KC, 0:KC]).then_inc(gains_in_psum, 1)

            def warm_up(n):
                for _ in range(n):
                    nc.tensor.transpose(acc[:, 2, 0:P], ident[:, :], ident[:, :])

            warm_up(4)
            for t in range(T):
                pe.wait_ge(x_loaded[t], 16)
                for bank in range(4):
                    for k in (2 * bank, 2 * bank + 1):
                        last = nc.tensor.transpose(aux[:, bank, (k % 2) * SEQ + t * P:(k % 2) * SEQ + (t + 1) * P],
                                                   x_sb[:, t, k * P:(k + 1) * P], ident[:, :])
                    if t == T - 1:
                        last.then_inc(xT_in_psum, 1)

            warm_up(8)

            def first_unit():
                for k in range(4):
                    pe.wait_ge(xT_hi_ready, k + 1)
                    pe.wait_ge(xT_lo_ready, k + 1)
                    pe.wait_ge(first_hi_ready, k + 1)
                    pe.wait_ge(first_lo_ready, k + 1)
                    for t in range(T):
                        last = product(acc[:, t, :], k, t, *weights(0, 512, k), k == 0, False)
                last.then_inc(unit_used, 1)

            def other_gains():
                pe.wait_ge(gains_ready, 1)
                pe.wait_ge(rows_loaded, 48)
                nc.tensor.transpose(acc[:, 3, 0:GAIN_ROWS - KC], other_rows[0:GAIN_ROWS - KC, :],
                                    ident[0:GAIN_ROWS - KC, 0:GAIN_ROWS - KC]).then_inc(gains_in_psum, 1)

            def gate_low():
                pe.wait_ge(low_hi_ready, 1)
                pe.wait_ge(low_lo_ready, 1)
                pe.wait_ge(xT_hi_ready, KC)
                pe.wait_ge(xT_lo_ready, KC)
                for k in range(KC):
                    left = w_hi[:, RING - 1, k * P:(k + 1) * P]
                    nc.tensor.matmul(acc[:, 2, 0:SEQ], left, aT_hi[:, k, :], start=k == 0, stop=False)
                    last = nc.tensor.matmul(acc[:, 2, 0:SEQ], left, aT_lo[:, k, :], start=False, stop=k == KC - 1)
                last.then_inc(low_in_psum, 1)

            def in_unit(u, midway=()):
                b, h = u // 2, u % 2
                unit_ready(u)
                if b == 1 and h == 0:
                    pe.wait_ge(lowT_ready, 1)
                    pe.wait_ge(gains_ready, 2)
                if b >= 2 and h == 0:
                    pe.wait_ge(block_ready, 2 * (b - 1))
                for t in range(T):
                    for k in range(4):
                        last = product(acc[:, 2 * (b % 2) + t, :], 4 * h + k, t, *weights(u % RING, 512, k),
                                       h == 0 and k == 0, h == 1 and k == 3)
                    if h == 1 and t == 0:
                        last.then_inc(tile0_in_psum, 1)
                    if t == 0:
                        for step in midway:
                            step()
                last.then_inc(unit_used, 1)

            def transposes(bank, blocks):
                for n, src in enumerate(blocks):
                    last = nc.tensor.transpose(aux[:, bank, n * P:(n + 1) * P], src, ident[:, :])
                return last

            def logits():
                pe.wait_ge(lowT_ready, 1)
                pe.wait_ge(up_loaded, 32)
                for t in range(T):
                    last = nc.tensor.matmul(aux[:, 1, t * QK:(t + 1) * QK], lowT[0:2 * RANK, t * P:(t + 1) * P],
                                            w_up[0:2 * RANK, :], start=True, stop=True)
                last.then_inc(logits_in_psum, 1)

            def cumulate():
                pe.wait_ge(log_a_ready, 1)
                pe.wait_ge(consts_built, 1)
                for t in range(T):
                    nc.tensor.matmul(aux[:, 2, t * QK:(t + 1) * QK], tri_cum[:, :], log_a[:, t, :], start=True, stop=True)
                    nc.tensor.matmul(aux[:, 3, t * QK:(t + 1) * QK], tri_rest[:, :], log_a[:, t, :], start=True, stop=True)
                    for pair in range(PAIRS):
                        c = pair * CHUNKS + 2 * t
                        last = nc.tensor.matmul(aux[:, 0, c:c + 2], log_a[:, t, pair * P:(pair + 1) * P],
                                                chunk_ind[:, :], start=True, stop=True)
                last.then_inc(cum_in_psum, 1)

            def gla_transposed():
                pe.wait_ge(gla_ops_ready, 2)
                for bank, src in ((1, q_dec), (2, k_inv)):
                    transposes(bank, [src[:, t, pair * P:(pair + 1) * P] for pair in range(PAIRS)
                                      for t in range(T)]).then_inc(glaT_in_psum, 1)

            def moba_transposed(which):
                pe.wait_ge(rotated, which + 1)
                if which == 1:
                    pe.wait_ge(mT_by_act, 1)
                    pe.wait_ge(mT_by_dve, 1)
                for n, bank in enumerate((3, 0)):
                    transposes(bank, [m_rot[:, which, t, h, :] for h in (2 * n, 2 * n + 1)
                                      for t in range(T)]).then_inc(mT_in_psum, 1)

            def gla_scores():
                pe.wait_ge(glaT_by_act, 2)
                pe.wait_ge(glaT_by_dve, 1)
                for t, bank in ((0, 1), (1, 2)):
                    tok = slice(t * P, (t + 1) * P)
                    for pair in range(PAIRS):
                        last = nc.tensor.matmul(aux[:, bank, pair * SEQ:(pair + 1) * SEQ], kiT[:, pair, tok],
                                                qdT[:, pair, :, tok], start=True, stop=True)
                    last.then_inc(a_in_psum, 1)

            def moba_scores():
                pe.wait_ge(mT_by_act, 2)
                pe.wait_ge(mT_by_dve, 2)
                pe.wait_ge(a_ready, 2)
                for h in range(HEADS):
                    last = nc.tensor.matmul(aux[:, 1, h * P:(h + 1) * P], mT[:, 0, h, 0:P], mT[:, 1, h, 0:P],
                                            start=True, stop=True)
                last.then_inc(scores_in_psum, 1)
                for h in range(HEADS):
                    last = nc.tensor.matmul(aux[:, 2 + h // 2, (h % 2) * SEQ:(h % 2 + 1) * SEQ], mT[:, 0, h, P:SEQ],
                                            mT[:, 1, h, :], start=True, stop=True)
                    if h % 2:
                        last.then_inc(scores_in_psum, 1)

            def probs_transposed():
                pe.wait_ge(probs_ready, 2)
                for bank, (s, k) in enumerate(((s_0, 0), (s_1, 0), (s_1, P))):
                    transposes(bank, [s[:, h, k:k + P] for h in range(HEADS)]).then_inc(probT_in_psum, 1)

            def moba_outputs():
                pe.wait_ge(probT_by_act, 2)
                pe.wait_ge(probT_by_dve, 1)
                pe.wait_ge(block_ready, 8)
                for t, bank in ((0, 3), (1, 0)):
                    for h in range(HEADS):
                        for k in range(t + 1):
                            last = nc.tensor.matmul(aux[:, bank, h * DV:(h + 1) * DV], probT[:, t + k, h, :],
                                                    mv[:, k, h * DV:(h + 1) * DV], start=k == 0, stop=k == t)
                    last.then_inc(moba_in_psum, 1)

            def gla_updates():
                pe.wait_ge(block_ready, 10)
                pe.wait_ge(gla_ops_ready, 3)
                for c in range(CHUNKS - 1):
                    t, rows = c // 2, slice((c % 2) * CHUNK, (c % 2 + 1) * CHUNK)
                    for h in range(HEADS):
                        pair, half = h // 2, slice((h % 2) * DK, (h % 2 + 1) * DK)
                        col = (c // 2) * PAIRS * DV + pair * DV
                        last = nc.tensor.matmul(aux[half, 1 + c % 2, col:col + DV],
                                                k_end[rows, t, h * DK:(h + 1) * DK], gv[rows, t, h * DV:(h + 1) * DV],
                                                start=True, stop=True)
                last.then_inc(update_in_psum, 1)

            def gla_outputs():
                pe.wait_ge(a_ready, 2)
                pe.wait_ge(states_ready, 1)
                for t in range(T):
                    for h in range(HEADS):
                        pair, par = h // 2, h % 2
                        cols = slice(h * DV, (h + 1) * DV)
                        nc.tensor.matmul(aux[:, 1 + t, cols], a_gla[:, t, h, :], gv[:, t, cols], start=True, stop=True)
                        for c in range(max(2 * t, 1), 2 * t + 2):
                            rows = slice((c % 2) * CHUNK, (c % 2 + 1) * CHUNK)
                            last = nc.tensor.matmul(aux[rows, 1 + t, cols],
                                                    qdT[:, pair, par, c * CHUNK:(c + 1) * CHUNK],
                                                    state[:, c - 1, pair, :], start=False, stop=True,
                                                    skip_group_check=True)
                    last.then_inc(gla_in_psum, 1)

            def heads_transposed(group, banks):
                for t, bank in enumerate(banks):
                    n = 2 * group + t
                    pe.wait_ge(heads_ready, n + 1)
                    o = (o_moba, o_gla)[group]
                    transposes(bank, [o[:, t, h, :] for h in range(HEADS)]).then_inc(headsT_in_psum, 1)

            def out_product(t, group, n):
                for k in range(4):
                    u = IN_UNITS + 2 * group + k // 2
                    last = product(acc[:, 2 * t + n, :], group * HEADS + k, t,
                                   *weights(u % RING, D, k % 2, 512 * n, 512 * n + 512),
                                   group == 0 and k == 0, group == 1 and k == 3)
                    if t == 1 and n == 1 and k % 2:
                        last.then_inc(unit_used, 1)
                if group == 1 and not (t == 1 and n == 1):
                    last.then_inc(mixed_in_psum, 1)

            def x2_transposed(part):
                t, n = part // 2, part % 2
                pe.wait_ge(x2_ready, part + 1)
                transposes(X2T_BANKS[part], [x_sb[:, t, k * P:(k + 1) * P]
                                             for k in range(4 * n, 4 * n + 4)]).then_inc(x2T_in_psum, 1)

            def gate_up(slot, h, t, parity, midway=None):
                for k in range(4):
                    last = product(aux[:, GATE_UP_BANKS[parity][t], :], 4 * h + k, t, *weights(slot, 512, k),
                                   h == 0 and k == 0, h == 1 and k == 3)
                    if k == 1 and midway is not None:
                        midway()
                if t == 1:
                    last.then_inc(unit_used, 1)
                elif h == 1:
                    last.then_inc(gu_in_psum, 1)

            def hidden_transposed(j):
                pe.wait_ge(hidden_ready, j * 2)
                if not isinstance(j, int) or j > 1:
                    pe.wait_ge(hiddenT_hi_ready, j - 1)
                    pe.wait_ge(hiddenT_lo_ready, j - 1)
                transposes(1, [hidden[:, t, k * P:(k + 1) * P] for k in range(2)
                               for t in range(T)]).then_inc(hiddenT_in_psum, 1)

            def down(slot, j, tiles=range(T), first=False, last=False):
                pe.wait_ge(hiddenT_hi_ready, j)
                pe.wait_ge(hiddenT_lo_ready, j)
                hi, lo = (aT_hi, aT_lo) if last else (pT_hi, pT_lo)
                for t in tiles:
                    for n in range(2):
                        for k in range(2):
                            ins = product(acc[:, 2 * t + n, :], k, t, *weights(slot, D, k, 512 * n, 512 * n + 512),
                                          first and k == 0, last and k == 1, hi, lo)
                        if last:
                            ins.then_inc(down_in_psum, 1)
                if not last and tiles[-1] == T - 1:
                    ins.then_inc(unit_used, 1)

            def gate_up_phase(j, u, slot, parity):
                unit_ready(u)
                gate_up(slot % RING, 0, 0, parity)
                hidden_transposed(j)
                gate_up(slot % RING, 0, 1, parity)
                unit_ready(u + 1)
                for t in range(T):
                    gate_up((slot + 1) % RING, 1, t, parity)

            def ffn_phase(j, u, slot, parity, first=False):
                gate_up_phase(j, u, slot, parity)
                unit_ready(u + 2)
                down((slot + 2) % RING, j, first=first)

            midway = {3: [cumulate], 6: [lambda: moba_transposed(0)], 7: [lambda: moba_transposed(1)],
                      9: [probs_transposed], 10: [gla_updates], 11: [lambda: heads_transposed(0, (3, 0)), gla_outputs]}
            after = {0: [gate_low, other_gains], 1: [logits], 4: [gla_transposed], 6: [gla_scores],
                     7: [moba_scores], 9: [moba_outputs]}
            for u in range(IN_UNITS):
                if u == 0:
                    first_unit()
                else:
                    in_unit(u, midway.get(u, ()))
                for step in after.get(u, ()):
                    step()

            for t in range(T):
                pe.wait_ge(headsT_hi_ready, t + 1)
                pe.wait_ge(headsT_lo_ready, t + 1)
                pe.wait_ge(block_ready, 10) if t == 0 else pe.wait_ge(silu_r_ready, 2)
                for n in range(2):
                    if t == 0 and n == 0:
                        unit_ready(IN_UNITS + 1)
                    if t == 1 and n == 1:
                        heads_transposed(1, (1, 2))
                    out_product(t, 0, n)
            unit_ready(IN_UNITS + 3)
            for t in range(T):
                pe.wait_ge(headsT_hi_ready, 2 + t + 1)
                pe.wait_ge(headsT_lo_ready, 2 + t + 1)
                for n in range(2):
                    out_product(t, 1, n)
                    if 2 * t + n > 0:
                        x2_transposed(2 * t + n - 1)

            for t in range(T):
                pe.wait_ge(x2T_hi_ready, (t + 1) * KC)
                pe.wait_ge(x2T_lo_ready, (t + 1) * KC)
                for h in range(2):
                    unit_ready(PHASE0 + h)
                    gate_up((PHASE0 + h) % RING, h, t, 0, (lambda: x2_transposed(3)) if t == 0 and h == 0 else None)

            ffn_phase(1, phase_unit(1), phase_unit(1), 1, first=True)
            with pe.Fori(0, LOOPED) as i:
                for a in range(2):
                    ffn_phase(i * 2 + (2 + a), i * 6 + phase_unit(2 + a), phase_unit(2 + a), a)
            j, u = PHASES - 1, phase_unit(PHASES - 1)
            gate_up_phase(j, u, u, j % 2)
            unit_ready(u + 2)
            down((u + 2) % RING, j, tiles=(0,))
            hidden_transposed(PHASES)
            down((u + 2) % RING, j, tiles=(1,))
            unit_ready(UNITS - 1)
            down((UNITS - 1) % RING, PHASES, last=True)

        @block.scalar
        def _(act):
            n_seq = [0]

            def then(ins):
                n_seq[0] += 1
                ins.then_inc(act_seq, 1)
                act.wait_ge(act_seq, n_seq[0])

            act.dma_start(gain_rows[0:KC, :], norm1_gain.rearrange("l (k p) -> (l k) p", p=P)).then_inc(norm1_loaded, 16)
            nc.scalar.preload_act_table(ACT.Exp)

            def split_as(slot, fills, used=None):
                act.wait_ge(raw_loaded[slot % RAW], fills * 32)
                if used is not None:
                    act.wait_ge(unit_used, used)
                nc.scalar.copy(w_hi[:, slot % RING, :], raw[:, slot % RAW, :]).then_inc(hi_ready, 1)

            def split(u):
                split_as(u, fill(u), u - RING + 1 if u >= RING else None)

            def sum_squares(norm, t):
                nc.scalar.activation(reuse_f[:, t * D:(t + 1) * D], x_sb[:, t, :], ACT.Square,
                                     accum_out=ss[:, norm, t:t + 1]).then_inc(ss_ready, 1)

            def take_block(b, dst):
                for t in range(T):
                    if t == 0:
                        act.wait_ge(tile0_in_psum, b + 1)
                    else:
                        act.wait_ge(unit_used, 2 * b + 2)
                    act.wait_ge(rstd_ready, t + 1)
                    nc.scalar.activation(dst[:, t], acc[:, 2 * (b % 2) + t, :], ACT.Copy,
                                         scale=rstd[:, 0, t:t + 1]).then_inc(block_ready, 1)

            def take_xT(chunks):
                for k in chunks:
                    act.wait_ge(xT_in_psum, k // 2 + 1)
                    nc.scalar.mul(aT_hi[:, k, :], aux[:, k // 2, (k % 2) * SEQ:(k % 2 + 1) * SEQ],
                                  gains[:, NORM1_ROW + k:NORM1_ROW + k + 1]).then_inc(xT_hi_ready, 1)

            def split_first(half):
                act.wait_ge(first_loaded[half], 16)
                for k in (2 * half, 2 * half + 1):
                    nc.scalar.copy(w_hi[:, 0, k * 512:(k + 1) * 512], raw[:, 0, k * 512:(k + 1) * 512]).then_inc(first_hi_ready, 1)

            act.wait_ge(gains_ready, 1)
            take_xT((0, 1))
            split_first(0)
            take_xT((2, 3))
            split_first(1)
            take_xT((4, 5, 6, 7))
            act.wait_ge(low_loaded, 16)
            nc.scalar.copy(low_w[:, :, :, 0, :], low_raw[:, :, :].unsqueeze(2).to_broadcast(LOW_COPIES)).then_inc(low_hi_ready, 1)
            split(1)
            for t in range(T):
                act.wait_ge(x_loaded[t], 16)
                sum_squares(0, t)
            split(2)
            split(3)
            take_block(0, gqk)
            act.wait_ge(logits_ready, 1)
            then(nc.scalar.activation(soft, log_a, ACT.Abs))
            then(nc.scalar.activation(soft, soft, ACT.Exp, scale=-1.0))
            nc.scalar.activation(soft, soft, ACT.Ln, bias=one[:, :]).then_inc(soft_ready, 1)
            nc.scalar.preload_act_table(ACT.Exp)
            split(4)
            act.wait_ge(low_in_psum, 1)
            split(5)
            act.wait_ge(cum_in_psum, 1)
            nc.scalar.activation(reuse_c[:, 0:512], aux[:, 2, :], ACT.Exp)
            nc.scalar.activation(reuse_c[:, 512:1024], aux[:, 2, :], ACT.Exp, scale=-1.0)
            nc.scalar.activation(reuse_c[:, 1024:1536], aux[:, 3, :], ACT.Exp)
            nc.scalar.activation(decay[:, :, :], aux[:, 0, 0:PAIRS * CHUNKS].rearrange("p (a c) -> p a c", a=PAIRS),
                                 ACT.Exp).then_inc(cum_exp_ready, 1)
            split(6)
            act.wait_ge(angles_ready, 1)
            act.wait_ge(consts_built, 1)
            nc.scalar.activation(sin_t[:, :, :], ang.rearrange("p (t d) -> p t d", t=T), ACT.Sin)
            nc.scalar.activation(cos_t[:, :, :], sin_arg.rearrange("p (t d) -> p t d", t=T), ACT.Sin,
                                 bias=half_pi[:, :], scale=-1.0).then_inc(sin_ready, 1)
            nc.scalar.preload_act_table(ACT.Exp)
            split(7)
            take_block(1, m_flat)
            split(8)
            act.wait_ge(glaT_in_psum, 1)
            nc.scalar.copy(qdT[0:DK, :, 0, :], aux[0:DK, 1, :].rearrange("p (a s) -> p a s", a=PAIRS)).then_inc(glaT_by_act, 1)
            act.wait_ge(glaT_in_psum, 2)
            nc.scalar.copy(kiT[:, :, :], aux[:, 2, :].rearrange("p (a s) -> p a s", a=PAIRS)).then_inc(glaT_by_act, 1)
            split(9)
            act.wait_ge(rotated, 1)
            take_block(2, m_flat)
            act.wait_ge(mT_in_psum, 1)
            nc.scalar.copy(mT[:, 0, 0:2, :], aux[:, 3, :].rearrange("p (h s) -> p h s", h=2)).then_inc(mT_by_act, 1)
            split(10)
            split(11)
            act.wait_ge(rotated, 2)
            act.wait_ge(mT_in_psum, 3)
            nc.scalar.copy(mT[:, 1, 0:2, :], aux[:, 3, :].rearrange("p (h s) -> p h s", h=2)).then_inc(mT_by_act, 1)
            split(12)
            take_block(3, mv)
            for t, s in ((0, s_0), (1, s_1)):
                act.wait_ge(max_ready, t + 1)
                for h in range(HEADS):
                    c = t * HEADS + h
                    last = nc.scalar.activation(s[:, h, :], s[:, h, :], ACT.Exp, bias=neg_max[:, c:c + 1], scale=SCALE,
                                                accum_out=row_sum[:, c:c + 1])
                last.then_inc(probs_ready, 1)
            nc.scalar.preload_act_table(ACT.Silu)
            split(13)
            for b in range(2):
                act.wait_ge(probT_in_psum, b + 1)
                nc.scalar.copy(probT[:, b, :, :], aux[:, b, :].rearrange("p (h q) -> p h q", h=HEADS)).then_inc(probT_by_act, 1)
            split(14)
            take_block(4, gv)
            for t, bank in ((0, 3), (1, 0)):
                act.wait_ge(moba_in_psum, t + 1)
                nc.scalar.activation(squares[:, t * W:(t + 1) * W], aux[:, bank, :], ACT.Square).then_inc(sq_ready, 1)
            split(15)
            split(16)
            def take_headsT(group, banks):
                row = (MOBA_ROW, GLA_ROW)[group]
                base = group * HEADS
                for t, bank in enumerate(banks):
                    act.wait_ge(headsT_in_psum, 2 * group + t + 1)
                    nc.scalar.mul(aT_hi[:, base:base + HEADS, t * P:(t + 1) * P],
                                  aux[:, bank, :].rearrange("p (h q) -> p h q", h=HEADS),
                                  gains[:, row:row + 1]).then_inc(headsT_hi_ready, 1)

            def take_r(t):
                nc.scalar.activation(silu_r[:, t, :, :], acc[:, 2 + t, :].rearrange("p (h v) -> p h v", h=HEADS), ACT.Silu,
                                     scale=rstd[:, 0, t:t + 1]).then_inc(silu_r_ready, 1)

            act.wait_ge(tile0_in_psum, len(BLOCKS))
            take_r(0)
            take_headsT(0, (3, 0))
            act.wait_ge(ms_h_ready, 1)
            for t in range(T):
                act.wait_ge(gla_in_psum, t + 1)
                nc.scalar.activation(squares[:, t * W:(t + 1) * W], aux[:, 1 + t, :], ACT.Square).then_inc(sq_ready, 1)
            act.wait_ge(unit_used, IN_UNITS)
            take_r(1)
            split(17)
            take_headsT(1, (1, 2))

            def take_x2T(t):
                for k in range(KC):
                    act.wait_ge(x2T_in_psum, 2 * t + k // 4 + 1)
                    nc.scalar.mul(aT_hi[:, k, t * P:(t + 1) * P], aux[:, X2T_BANKS[2 * t + k // 4], (k % 4) * P:(k % 4 + 1) * P],
                                  gains[:, NORM2_ROW + k:NORM2_ROW + k + 1]).then_inc(x2T_hi_ready, 1)

            def take_gate(j, u, parity):
                for t in range(T):
                    if t == 0:
                        act.wait_ge(gu_in_psum, j + 1)
                    else:
                        act.wait_ge(unit_used, u + 2)
                    if isinstance(j, int):
                        act.wait_ge(rstd_ready, T + t + 1)
                    nc.scalar.activation(silu_g[:, t, :], aux[:, GATE_UP_BANKS[parity][t], 0:FF], ACT.Silu,
                                         scale=rstd[:, 1, t:t + 1]).then_inc(silu_ready, 1)

            split(18)
            split(19)
            take_x2T(0)
            sum_squares(1, 0)
            take_x2T(1)
            sum_squares(1, 1)
            split(20)
            take_gate(0, PHASE0, 0)

            def take_hiddenT(dst):
                nc.scalar.copy(dst, aux[:, 1, :].rearrange("p (k s) -> p k s", k=2)).then_inc(hiddenT_hi_ready, 1)

            def ffn_phase(j, u, fills, slot, parity, n_units=3):
                act.wait_ge(hiddenT_in_psum, j)
                act.wait_ge(unit_used, u)
                take_hiddenT(pT_hi[:, :, :])
                for n in range(n_units):
                    split_as(slot + 3 + n, fills - (0 if (slot + n) % RAW else 1), u + (n + 4 - RING))
                take_gate(j, u, parity)

            ffn_phase(1, phase_unit(1), fill(phase_unit(2) + 1), phase_unit(1), 1)
            with act.Fori(0, LOOPED) as i:
                for a in range(2):
                    ffn_phase(i * 2 + (2 + a), i * 6 + phase_unit(2 + a), i * 2 + fill(phase_unit(3 + a) + 1),
                              phase_unit(2 + a), a)
            ffn_phase(PHASES - 1, phase_unit(PHASES - 1), fill(phase_unit(PHASES) + 1), phase_unit(PHASES - 1),
                      (PHASES - 1) % 2, n_units=1)
            act.wait_ge(hiddenT_in_psum, PHASES)
            take_hiddenT(aT_hi[:, 0:2, :])

            def x3_squares(n):
                t, cols = n // 2, slice((n % 2) * 512, (n % 2 + 1) * 512)
                act.wait_ge(x3_ready, n + 1)
                nc.scalar.activation(reuse_f[:, n * 512:(n + 1) * 512], x_sb[:, t, cols], ACT.Square,
                                     accum_out=ss_f[:, t, n % 2:n % 2 + 1]).then_inc(x3_sums_ready, 1)

            def out_right(t):
                act.wait_ge(rstd_ready, 2 * T + t + 1)
                act.wait_ge(gained, 2 * t + 2)
                nc.scalar.mul(out_sb[:, t, 512:D], out_sb[:, t, 512:D], rstd[:, 2, t:t + 1]).then_inc(out_right_ready, 1)

            for n in range(3):
                x3_squares(n)
            out_right(0)
            x3_squares(3)
            out_right(1)

        @block.vector
        def _(dve):
            n_seq = [0]

            def then(ins):
                n_seq[0] += 1
                ins.then_inc(dve_seq, 1)
                dve.wait_ge(dve_seq, n_seq[0])

            def split(u, slot=None):
                slot = u if slot is None else slot
                dve.wait_ge(hi_ready, u)
                nc.vector.tensor_tensor(w_lo[:, slot % RING, :], raw[:, slot % RAW, :],
                                        w_hi[:, slot % RING, :].bitcast(f32), ALU.subtract).then_inc(lo_ready, 1)

            def lo_of_scaled(out_lo, src, gain, hi):
                return nc.vector.scalar_tensor_tensor(out=out_lo, in0=src, scalar=gain, in1=hi.bitcast(f32),
                                                      op0=ALU.mult, op1=ALU.subtract)

            def take_xT(chunks):
                for k in chunks:
                    dve.wait_ge(xT_hi_ready, k // 2 * 2 + 2)
                    lo_of_scaled(aT_lo[:, k, :], aux[:, k // 2, (k % 2) * SEQ:(k % 2 + 1) * SEQ],
                                 gains[:, NORM1_ROW + k:NORM1_ROW + k + 1], aT_hi[:, k, :]).then_inc(xT_lo_ready, 1)

            def split_first(k):
                dve.wait_ge(first_hi_ready, k + 1)
                cols = slice(k * 512, (k + 1) * 512)
                nc.vector.tensor_tensor(w_lo[:, 0, cols], raw[:, 0, cols], w_hi[:, 0, cols].bitcast(f32),
                                        ALU.subtract).then_inc(first_lo_ready, 1)

            dve.wait_ge(gains_in_psum, 1)
            nc.vector.tensor_copy(gains[:, 0:KC], acc[:, 3, 0:KC]).then_inc(gains_ready, 1)
            dve.wait_ge(gains_ready, 1)
            for k in range(4):
                take_xT((k,))
                split_first(k)
            take_xT((4, 5, 6, 7))
            split(1)
            dve.wait_ge(low_in_psum, 1)
            nc.vector.tensor_copy(lowT[0:2 * RANK, :], acc[0:2 * RANK, 2, 0:SEQ]).then_inc(lowT_ready, 1)
            dve.wait_ge(gains_in_psum, 2)
            nc.vector.tensor_copy(gains[:, KC:GAIN_ROWS], acc[:, 3, 0:GAIN_ROWS - KC]).then_inc(gains_ready, 1)
            split(2)
            split(3)
            dve.wait_ge(logits_in_psum, 1)
            dve.wait_ge(rstd_ready, T)
            dve.wait_ge(bias_loaded, 16)
            for t in range(T):
                last = nc.vector.scalar_tensor_tensor(out=log_a[:, t, :], in0=aux[:, 1, t * QK:(t + 1) * QK],
                                                      scalar=rstd[:, 0, t:t + 1], in1=gate_bias, op0=ALU.mult, op1=ALU.add)
            last.then_inc(logits_ready, 1)
            dve.wait_ge(pos_loaded, 32)
            then(nc.vector.tensor_copy(pos_f[:, :], pos_i[:, :]))
            for t in range(T):
                last = nc.vector.tensor_scalar(ang[:, t * HALF:(t + 1) * HALF], freq[:, :], pos_f[:, t:t + 1], None, ALU.mult)
            then(last)

            def nearest_turns():
                then(nc.vector.tensor_scalar(turns, ang, 1.0 / (2.0 * np.pi), MAGIC, ALU.mult, ALU.add))
                then(nc.vector.tensor_scalar(turns, turns, -MAGIC, None, ALU.add))

            def take_off(n, part):
                then(nc.vector.scalar_tensor_tensor(out=ang, in0=n, scalar=-part, in1=ang, op0=ALU.mult, op1=ALU.add))

            nearest_turns()
            then(nc.vector.tensor_copy(turns_hi, turns))
            then(nc.vector.tensor_tensor(turns_lo, turns, turns_hi.bitcast(f32), ALU.subtract))
            for part in two_pi_parts(5):
                take_off(turns_hi.bitcast(f32), part)
                take_off(turns_lo, part)
            dve.wait_ge(soft_ready, 1)
            nc.vector.scalar_tensor_tensor(out=log_a, in0=log_a, scalar=0.0, in1=soft, op0=ALU.min,
                                           op1=ALU.subtract).then_inc(log_a_ready, 1)
            nearest_turns()
            for part in two_pi_parts(3):
                take_off(turns, part)
            then(nc.vector.tensor_scalar(ang, ang, PI_BELOW, -PI_BELOW, ALU.min, ALU.max))
            nc.vector.scalar_tensor_tensor(out=sin_arg, in0=ang, scalar=-1.0, in1=ang, op0=ALU.mult, op1=ALU.max).then_inc(angles_ready, 1)
            split(4)
            split(5)

            def rotate(which):
                dve.wait_ge(block_ready, 4 + 2 * which)
                dve.wait_ge(sin_ready, 1)
                cos, sin = (v[:, :, :].unsqueeze(2).to_broadcast([P, T, HEADS, HALF]) for v in (cos_t, sin_t))
                a, b = m_raw[:, :, :, 0:HALF], m_raw[:, :, :, HALF:DV]
                out_a, out_b = m_rot[:, which, :, :, 0:HALF], m_rot[:, which, :, :, HALF:DV]
                nc.vector.tensor_tensor(out_a, a, cos, ALU.mult)
                nc.vector.tensor_tensor(out_b, b, cos, ALU.mult)
                then(nc.vector.tensor_tensor(rot_tmp, b, sin, ALU.mult))
                then(nc.vector.tensor_tensor(out_a, out_a, rot_tmp, ALU.subtract))
                then(nc.vector.tensor_tensor(rot_tmp, a, sin, ALU.mult))
                nc.vector.tensor_tensor(out_b, out_b, rot_tmp, ALU.add).then_inc(rotated, 1)

            dve.wait_ge(cum_exp_ready, 1)
            dve.wait_ge(block_ready, 2)
            nc.vector.scalar_tensor_tensor(out=q_dec, in0=gqk[:, :, 0:QK], scalar=float(DK) ** -0.5, in1=q_dec,
                                           op0=ALU.mult, op1=ALU.mult).then_inc(gla_ops_ready, 1)
            nc.vector.tensor_tensor(k_inv, gqk[:, :, QK:2 * QK], k_inv, ALU.mult).then_inc(gla_ops_ready, 1)
            nc.vector.tensor_tensor(k_end, gqk[:, :, QK:2 * QK], k_end, ALU.mult).then_inc(gla_ops_ready, 1)
            split(6)
            split(7)
            rotate(0)
            split(8)
            dve.wait_ge(glaT_in_psum, 1)
            nc.vector.tensor_copy(qdT[DK:P, :, 1, :], aux[DK:P, 1, :].rearrange("p (a s) -> p a s", a=PAIRS)).then_inc(glaT_by_dve, 1)
            split(9)
            dve.wait_ge(mT_in_psum, 2)
            nc.vector.tensor_copy(mT[:, 0, 2:4, :], aux[:, 0, :].rearrange("p (h s) -> p h s", h=2)).then_inc(mT_by_dve, 1)
            rotate(1)
            dve.wait_ge(a_zeroed, 1)
            dve.wait_ge(consts_built, 1)
            mask = gla_mask[:, :].bitcast(i32).unsqueeze(1).to_broadcast([P, HEADS, P])
            for t, bank in ((0, 1), (1, 2)):
                dve.wait_ge(a_in_psum, t + 1)
                nc.vector.copy_predicated(a_gla[:, t, :, :], mask,
                                          aux[:, bank, :].rearrange("p (h s) -> p h s", h=HEADS)).then_inc(a_ready, 1)
            dve.wait_ge(mT_in_psum, 4)
            nc.vector.tensor_copy(mT[:, 1, 2:4, :], aux[:, 0, :].rearrange("p (h s) -> p h s", h=2)).then_inc(mT_by_dve, 1)
            split(10)
            dve.wait_ge(scores_in_psum, 1)
            then(nc.vector.tensor_tensor(s_0, aux[:, 1, :].rearrange("p (h k) -> p h k", h=HEADS),
                                         causal[:, P:2 * P].unsqueeze(1).to_broadcast([P, HEADS, P]), ALU.add))
            then(nc.vector.reduce_max(row_max[:, 0:HEADS], s_0, AX.X))
            nc.vector.tensor_scalar(neg_max[:, 0:HEADS], row_max[:, 0:HEADS], -SCALE, None, ALU.mult).then_inc(max_ready, 1)
            for n in range(2):
                dve.wait_ge(scores_in_psum, n + 2)
                last = nc.vector.tensor_tensor(s_1[:, 2 * n:2 * n + 2, :], aux[:, 2 + n, :].rearrange("p (h k) -> p h k", h=2),
                                               causal[:, :].unsqueeze(1).to_broadcast([P, 2, 2 * P]), ALU.add)
            then(last)
            then(nc.vector.reduce_max(row_max[:, HEADS:2 * HEADS], s_1, AX.X))
            nc.vector.tensor_scalar(neg_max[:, HEADS:2 * HEADS], row_max[:, HEADS:2 * HEADS], -SCALE, None,
                                    ALU.mult).then_inc(max_ready, 1)
            split(11)
            split(12)
            dve.wait_ge(probT_in_psum, 3)
            nc.vector.tensor_copy(probT[:, 2, :, :], aux[:, 2, :].rearrange("p (h q) -> p h q", h=HEADS)).then_inc(probT_by_dve, 1)
            split(13)
            split(14)

            def head_squares(group):
                dve.wait_ge(sq_ready, 2 * group + 2)
                then(nc.vector.reduce_sum(ss_h[:, group, :], squares.rearrange("p (c v) -> p c v", v=DV), AX.X))

            def normed(group, t, bank, dst):
                factor = rstd_h[:, group, t * HEADS:(t + 1) * HEADS].unsqueeze(2).to_broadcast([P, HEADS, DV])
                return nc.vector.tensor_tensor(dst, aux[:, bank, :].rearrange("p (h v) -> p h v", h=HEADS), factor, ALU.mult)

            dve.wait_ge(probs_ready, 2)
            then(nc.vector.scalar_tensor_tensor(out=l2_h[:, :], in0=row_sum[:, :], scalar=EPS, in1=row_sum[:, :],
                                                op0=ALU.mult, op1=ALU.mult))
            head_squares(0)
            nc.vector.scalar_tensor_tensor(out=ms_h[:, 0, :], in0=ss_h[:, 0, :], scalar=1.0 / DV, in1=l2_h[:, :],
                                           op0=ALU.mult, op1=ALU.add).then_inc(ms_h_ready, 1)
            dve.wait_ge(update_in_psum, 1)

            def update(c):
                col = (c // 2) * PAIRS * DV
                return aux[:, 1 + c % 2, col:col + PAIRS * DV].rearrange("p (a v) -> p a v", a=PAIRS)

            then(nc.vector.tensor_copy(state[:, 0, :, :], update(0)))
            for c in range(1, CHUNKS - 1):
                for pair in range(PAIRS):
                    last = nc.vector.scalar_tensor_tensor(out=state[:, c, pair, :], in0=state[:, c - 1, pair, :],
                                                          scalar=decay[:, pair, c:c + 1], in1=update(c)[:, pair, :],
                                                          op0=ALU.mult, op1=ALU.add)
                if c < CHUNKS - 2:
                    then(last)
            last.then_inc(states_ready, 1)
            dve.wait_ge(rstd_h_ready, 1)
            for t, bank in ((0, 3), (1, 0)):
                normed(0, t, bank, o_moba[:, t, :, :]).then_inc(heads_ready, 1)
            split(15)
            split(16)

            def take_headsT(group, banks):
                row = (MOBA_ROW, GLA_ROW)[group]
                base = group * HEADS
                for t, bank in enumerate(banks):
                    dve.wait_ge(headsT_hi_ready, 2 * group + t + 1)
                    dst = slice(base, base + HEADS), slice(t * P, (t + 1) * P)
                    lo_of_scaled(aT_lo[:, dst[0], dst[1]], aux[:, bank, :].rearrange("p (h q) -> p h q", h=HEADS),
                                 gains[:, row:row + 1], aT_hi[:, dst[0], dst[1]]).then_inc(headsT_lo_ready, 1)

            take_headsT(0, (3, 0))
            head_squares(1)
            nc.vector.tensor_scalar(ms_h[:, 1, :], ss_h[:, 1, :], 1.0 / DV, EPS, ALU.mult, ALU.add).then_inc(ms_h_ready, 1)
            dve.wait_ge(rstd_h_ready, 2)
            dve.wait_ge(silu_r_ready, 2)
            normed(1, 0, 1, o_gla[:, 0, :, :])
            then(normed(1, 1, 2, o_gla[:, 1, :, :]))
            for t in range(T):
                nc.vector.tensor_tensor(o_gla[:, t, :, :], o_gla[:, t, :, :], silu_r[:, t, :, :], ALU.mult).then_inc(heads_ready, 1)
            split(17)
            take_headsT(1, (1, 2))

            def residual(t, n, ready):
                cols = slice(512 * n, 512 * n + 512)
                nc.vector.tensor_tensor(x_sb[:, t, cols], acc[:, 2 * t + n, :], x_sb[:, t, cols], ALU.add).then_inc(ready, 1)

            def take_x2T(t):
                for k in range(KC):
                    dve.wait_ge(x2T_hi_ready, t * KC + k // 4 * 4 + 4)
                    tok = slice(t * P, (t + 1) * P)
                    lo_of_scaled(aT_lo[:, k, tok], aux[:, X2T_BANKS[2 * t + k // 4], (k % 4) * P:(k % 4 + 1) * P],
                                 gains[:, NORM2_ROW + k:NORM2_ROW + k + 1], aT_hi[:, k, tok]).then_inc(x2T_lo_ready, 1)

            for n in range(2):
                dve.wait_ge(mixed_in_psum, n + 1)
                residual(0, n, x2_ready)
            split(18)
            dve.wait_ge(mixed_in_psum, 3)
            residual(1, 0, x2_ready)
            take_x2T(0)
            dve.wait_ge(unit_used, PHASE0)
            residual(1, 1, x2_ready)
            take_x2T(1)
            split(19)
            split(20)

            def take_up(j, parity):
                for t in range(T):
                    dve.wait_ge(silu_ready, j * 2 + (t + 1))
                    nc.vector.scalar_tensor_tensor(out=hidden[:, t, :], in0=aux[:, GATE_UP_BANKS[parity][t], FF:2 * FF],
                                                   scalar=rstd[:, 1, t:t + 1], in1=silu_g[:, t, :],
                                                   op0=ALU.mult, op1=ALU.mult).then_inc(hidden_ready, 1)

            def take_hiddenT(j, hi, lo):
                dve.wait_ge(hiddenT_hi_ready, j)
                nc.vector.tensor_tensor(lo, aux[:, 1, :].rearrange("p (k s) -> p k s", k=2), hi.bitcast(f32),
                                        ALU.subtract).then_inc(hiddenT_lo_ready, 1)

            def ffn_phase(j, u, slot, parity, n_units=3):
                take_hiddenT(j, pT_hi[:, :, :], pT_lo[:, :, :])
                for n in range(n_units):
                    split(u + 3 + n, slot + 3 + n)
                take_up(j, parity)

            take_up(0, 0)
            ffn_phase(1, phase_unit(1), phase_unit(1), 1)
            with dve.Fori(0, LOOPED) as i:
                for a in range(2):
                    ffn_phase(i * 2 + (2 + a), i * 6 + phase_unit(2 + a), phase_unit(2 + a), a)
            ffn_phase(PHASES - 1, phase_unit(PHASES - 1), phase_unit(PHASES - 1), (PHASES - 1) % 2, n_units=1)
            take_hiddenT(PHASES, aT_hi[:, 0:2, :], aT_lo[:, 0:2, :])

            def x3_part(n):
                dve.wait_ge(down_in_psum, n + 1)
                residual(n // 2, n % 2, x3_ready)

            def gain_part(n):
                t, cols = n // 2, slice((n % 2) * 512, (n % 2 + 1) * 512)
                dve.wait_ge(x3_ready, n + 1)
                nc.vector.tensor_tensor(out_sb[:, t, cols], x_sb[:, t, cols], gain_f[:, cols], ALU.mult).then_inc(gained, 1)

            def out_left(t):
                dve.wait_ge(rstd_ready, 2 * T + t + 1)
                dve.wait_ge(gained, 2 * t + 1)
                nc.vector.tensor_scalar(out_sb[:, t, 0:512], out_sb[:, t, 0:512], rstd[:, 2, t:t + 1], None,
                                        ALU.mult).then_inc(out_left_ready, 1)

            dve.wait_ge(gain_f_loaded, 16)
            for n in range(3):
                x3_part(n)
                gain_part(n)
            x3_part(3)
            out_left(0)
            gain_part(3)
            out_left(1)


_INS = ["x", "positions", "norm1_gain", "w_in", "w_gate_up", "b_gate", "gla_out_gain", "moba_out_gain", "w_out",
        "norm2_gain", "w_ffn_gate", "w_ffn_up", "w_ffn_down", "final_norm_gain"]


def kernel(**inputs):
    import numpy as _np
    import concourse.bacc as _bacc
    from concourse import mybir as _mybir
    from concourse.bass_utils import run_bass_kernel_spmd as _run

    nc = _bacc.Bacc("TRN2", target_bir_lowering=False, num_devices=1)
    arrays = {name: _np.ascontiguousarray(inputs[name]) for name in _INS}
    arrays["inv_freq"] = _np.power(_np.float32(ROPE_THETA), -_np.arange(HALF, dtype=_np.float32) / HALF)[None].astype(_np.float32)
    args = [nc.dram_tensor(f"in_{name}", a.shape, _mybir.dt.from_np(a.dtype), kind="ExternalInput").ap()
            for name, a in arrays.items()]
    out = nc.dram_tensor("out", (1, SEQ, D), _mybir.dt.float32, kind="ExternalOutput").ap()
    build_block(nc, *args, out)
    r = _run(nc, [{f"in_{name}": a for name, a in arrays.items()}], core_ids=[0])
    return r.results[0]["out"]
```
